# Optimizing a Trainium2 kernel written in Bass

```python
import jax, jax.numpy as jnp
from jax import lax
import numpy as np

D_MODEL = 1024
BATCH = 1
SEQ = 256
DEPTH = 2

CHUNK = 64
RET_HEADS = 4
RET_QK_DIM = D_MODEL // RET_HEADS
RET_V_WIDTH = 2 * D_MODEL
RET_V_DIM = RET_V_WIDTH // RET_HEADS
CONV_WIDTH = D_MODEL
CONV_KERNEL = 31
N_BRANCHES = 2
IN_COLS = 2 * D_MODEL + 2 * RET_V_WIDTH + 2 * CONV_WIDTH + N_BRANCHES * D_MODEL
SPLITS = (
    D_MODEL,
    2 * D_MODEL,
    2 * D_MODEL + RET_V_WIDTH,
    2 * D_MODEL + 2 * RET_V_WIDTH,
    2 * D_MODEL + 2 * RET_V_WIDTH + CONV_WIDTH,
    2 * D_MODEL + 2 * RET_V_WIDTH + 2 * CONV_WIDTH,
)
D_FF = 2816
N_EXPERTS = 8
TOP_K = 2
EXPERT_D_FF = 1408
N_DENSE = (DEPTH + 1) // 2
N_MOE = DEPTH // 2
ROPE_BASE = 10000.0
EPS = 1e-6

kernel_name = "hybrid_retention_conformer_moe_trunk"

def rmsnorm(x, g):
    xf = x.astype(jnp.float32)
    y = xf * lax.rsqrt(jnp.mean(xf * xf, axis=-1, keepdims=True) + EPS)
    return (y * g.astype(jnp.float32)).astype(x.dtype)

def layernorm(x, g, b):
    xf = x.astype(jnp.float32)
    mu = jnp.mean(xf, axis=-1, keepdims=True)
    xc = xf - mu
    y = xc * lax.rsqrt(jnp.mean(xc * xc, axis=-1, keepdims=True) + EPS)
    return (y * g.astype(jnp.float32) + b.astype(jnp.float32)).astype(x.dtype)

def rotary(t, pos):
    half = t.shape[-1] // 2
    inv_freq = ROPE_BASE ** (-jnp.arange(half, dtype=jnp.float32) / half)
    ang = pos[:, None] * inv_freq[None, :]
    cos = jnp.cos(ang)[None, :, None, :]
    sin = jnp.sin(ang)[None, :, None, :]
    tf = t.astype(jnp.float32)
    t1, t2 = tf[..., :half], tf[..., half:]
    out = jnp.concatenate([t1 * cos - t2 * sin, t1 * sin + t2 * cos], axis=-1)
    return out.astype(t.dtype)

def retention(q, k, v):
    b, s, h, dk = q.shape
    dv = v.shape[-1]
    n = s // CHUNK
    log_g = jnp.log1p(-jnp.exp2(-5.0 - jnp.arange(h, dtype=jnp.float32)))

    def to_chunks(t):
        return t.astype(jnp.float32).reshape(b, n, CHUNK, h, t.shape[-1]).transpose(0, 3, 1, 2, 4)

    qc, kc, vc = to_chunks(q), to_chunks(k), to_chunks(v)
    idx = jnp.arange(CHUNK, dtype=jnp.float32)
    intra_decay = jnp.exp(log_g[:, None, None] * jnp.abs(idx[:, None] - idx[None, :]))
    scores = jnp.einsum('bhnid,bhnjd->bhnij', qc, kc) * intra_decay[None, :, None]
    intra = jnp.einsum('bhnij,bhnje->bhnie', scores, vc)

    q_decay = jnp.exp(log_g[:, None] * (idx[None, :] + 1.0))
    k_decay = jnp.exp(log_g[:, None] * (CHUNK - 1.0 - idx[None, :]))
    chunk_decay = jnp.exp(log_g * CHUNK)

    def step(state, inp):
        qn, kn, vn = inp
        cross = jnp.einsum('bhid,bhde->bhie', qn, state) * q_decay[None, :, :, None]
        kv = jnp.einsum('bhjd,bhje->bhde', kn * k_decay[None, :, :, None], vn)
        state = state * chunk_decay[None, :, None, None] + kv
        return state, cross

    xs = (qc.transpose(2, 0, 1, 3, 4), kc.transpose(2, 0, 1, 3, 4), vc.transpose(2, 0, 1, 3, 4))
    state0 = jnp.zeros((b, h, dk, dv), jnp.float32)
    _, cross = lax.scan(step, state0, xs)
    out = intra + cross.transpose(1, 2, 0, 3, 4)
    return out.transpose(0, 2, 3, 1, 4).reshape(b, s, h, dv)

def mixer(x, norm_g, w_in, b_gate, conv_w, conv_b, conv_ln_g, conv_ln_b,
          w_ret_o, w_conv_o, b_conv_o, w_out):
    b, s, _ = x.shape
    hn = rmsnorm(x, norm_g)
    proj = hn @ w_in
    q, k, v, g_ret_out, glu_val, glu_gate, gate_logits = jnp.split(proj, SPLITS, axis=-1)

    pos = jnp.arange(s, dtype=jnp.float32)
    q = rotary(q.reshape(b, s, RET_HEADS, RET_QK_DIM), pos)
    k = rotary(k.reshape(b, s, RET_HEADS, RET_QK_DIM), pos) * (RET_QK_DIM ** -0.5)
    v = v.reshape(b, s, RET_HEADS, RET_V_DIM)
    r = retention(q, k, v)
    r = r * lax.rsqrt(jnp.mean(r * r, axis=-1, keepdims=True) + EPS)
    r = (jax.nn.silu(g_ret_out.astype(jnp.float32)) * r.reshape(b, s, RET_V_WIDTH)).astype(x.dtype)
    branch_ret = r @ w_ret_o

    u = glu_val * jax.nn.sigmoid(glu_gate)
    u = lax.conv_general_dilated(
        u, conv_w[:, None, :], window_strides=(1,), padding=[(CONV_KERNEL - 1, 0)],
        dimension_numbers=('NWC', 'WIO', 'NWC'), feature_group_count=CONV_WIDTH) + conv_b
    u = jax.nn.silu(layernorm(u, conv_ln_g, conv_ln_b))
    branch_conv = u @ w_conv_o + b_conv_o

    gates = jax.nn.sigmoid(gate_logits + b_gate)
    g_a, g_b = jnp.split(gates, N_BRANCHES, axis=-1)
    merged = g_a * branch_ret + g_b * branch_conv
    return merged @ w_out

def swiglu(h, w1, w3, w2):
    return (jax.nn.silu(h @ w1) * (h @ w3)) @ w2

def moe(h, router, w1, w3, w2):
    logits = (h @ router).astype(jnp.float32)
    top_val, top_idx = lax.top_k(logits, TOP_K)
    top_w = jax.nn.softmax(top_val, axis=-1)
    gate = jnp.sum(jax.nn.one_hot(top_idx, N_EXPERTS, dtype=jnp.float32) * top_w[..., None], axis=-2)
    gate = gate.astype(h.dtype)
    out = jnp.zeros_like(h)
    for e in range(N_EXPERTS):
        out = out + gate[..., e:e + 1] * swiglu(h, w1[e], w3[e], w2[e])
    return out

def setup_inputs(seed: int = 0) -> dict:
    key = jax.random.key(seed)
    ks = jax.random.split(key, 24)
    f32 = jnp.float32
    D = D_MODEL

    def nrm(k, shape, fan_in):
        return jax.random.normal(k, shape, f32) * (fan_in ** -0.5)

    def gain(k, shape):
        return 1.0 + 0.01 * jax.random.normal(k, shape, f32)

    def small(k, shape):
        return 0.01 * jax.random.normal(k, shape, f32)

    return {
        "x": jax.random.normal(ks[0], (BATCH, SEQ, D), f32),
        "mix_norm": gain(ks[1], (DEPTH, D)),
        "w_in": nrm(ks[2], (DEPTH, D, IN_COLS), D),
        "b_gate": small(ks[3], (DEPTH, N_BRANCHES * D)),
        "conv_w": nrm(ks[4], (DEPTH, CONV_KERNEL, CONV_WIDTH), CONV_KERNEL),
        "conv_b": small(ks[5], (DEPTH, CONV_WIDTH)),
        "conv_ln_g": gain(ks[6], (DEPTH, CONV_WIDTH)),
        "conv_ln_b": small(ks[7], (DEPTH, CONV_WIDTH)),
        "w_ret_o": nrm(ks[8], (DEPTH, RET_V_WIDTH, D), RET_V_WIDTH),
        "w_conv_o": nrm(ks[9], (DEPTH, CONV_WIDTH, D), CONV_WIDTH),
        "b_conv_o": small(ks[10], (DEPTH, D)),
        "w_out": nrm(ks[11], (DEPTH, D, D), D),
        "ffn_norm": gain(ks[12], (DEPTH, D)),
        "dense_w1": nrm(ks[13], (N_DENSE, D, D_FF), D),
        "dense_w3": nrm(ks[14], (N_DENSE, D, D_FF), D),
        "dense_w2": nrm(ks[15], (N_DENSE, D_FF, D), D_FF),
        "moe_router": nrm(ks[16], (N_MOE, D, N_EXPERTS), D),
        "moe_w1": nrm(ks[17], (N_MOE, N_EXPERTS, D, EXPERT_D_FF), D),
        "moe_w3": nrm(ks[18], (N_MOE, N_EXPERTS, D, EXPERT_D_FF), D),
        "moe_w2": nrm(ks[19], (N_MOE, N_EXPERTS, EXPERT_D_FF, D), EXPERT_D_FF),
        "final_norm": gain(ks[20], (D,)),
    }

def reference(x, mix_norm, w_in, b_gate, conv_w, conv_b, conv_ln_g, conv_ln_b,
              w_ret_o, w_conv_o, b_conv_o, w_out, ffn_norm,
              dense_w1, dense_w3, dense_w2, moe_router, moe_w1, moe_w3, moe_w2,
              final_norm):
    for i in range(DEPTH):
        x = x + mixer(x, mix_norm[i], w_in[i], b_gate[i], conv_w[i], conv_b[i],
                      conv_ln_g[i], conv_ln_b[i], w_ret_o[i], w_conv_o[i],
                      b_conv_o[i], w_out[i])
        hn = rmsnorm(x, ffn_norm[i])
        j = i // 2
        if i % 2 == 0:
            x = x + swiglu(hn, dense_w1[j], dense_w3[j], dense_w2[j])
        else:
            x = x + moe(hn, moe_router[j], moe_w1[j], moe_w3[j], moe_w2[j])
    return rmsnorm(x, final_norm)


_drawn_inputs = setup_inputs


def setup_inputs(seed=0):
    import zlib

    import numpy as np

    out = dict(_drawn_inputs(seed))
    spreads = {}
    factors = {'mix_norm': 2.778,
     'b_gate': 8.0,
     'conv_b': 3.845,
     'conv_ln_g': 16.241,
     'conv_ln_b': 16.316,
     'final_norm': 34.851,
     'b_conv_o': 6.692,
     'ffn_norm': 6.305}
    for name, (base, spread) in spreads.items():
        noise = np.random.default_rng([zlib.crc32(name.encode()), seed]).standard_normal(out[name].shape)
        drawn = base * np.exp(spread * noise) if base else spread * noise
        out[name] = __import__('jax').numpy.asarray(drawn.astype(out[name].dtype))
    for name, factor in factors.items():
        out[name] = (out[name] * factor).astype(out[name].dtype)
    return out
```

```python
from contextlib import ExitStack

import numpy as np

import concourse.bass as bass
from concourse import mybir

P = 128
D = 1024
T = 256
DEPTH = 2
KC = D // P
TT = T // P
HEADS = 4
QKD = D // HEADS
VW = 2 * D
VD = VW // HEADS
VC = VW // P
CHUNK = 64
TAPS = 31
PAD = TAPS - 1
DFF = 2816
NEXP = 8
EFF = 1408
EPS = 1e-6

UNIT = 8 * P
RING = 4
N_GLU, N_QK, N_V, N_G, N_MG, N_RO, N_CO, N_WO = 16, 16, 16, 16, 16, 16, 8, 8
GLU0 = 0
QK0 = GLU0 + N_GLU
V0 = QK0 + N_QK
G0 = V0 + N_V
MG0 = G0 + N_G
RO0 = MG0 + N_MG
CO0 = RO0 + N_RO
WO0 = CO0 + N_CO
MIXER_UNITS = WO0 + N_WO
DENSE_CHUNKS = DFF // P
MOE_CHUNKS = NEXP * EFF // P
EXP_CHUNKS = EFF // P
FFN_CHUNKS = (DENSE_CHUNKS, MOE_CHUNKS)
LAYER0 = (0, MIXER_UNITS + 3 * DENSE_CHUNKS)
UNITS = LAYER0[1] + MIXER_UNITS + 3 * MOE_CHUNKS

F32 = mybir.dt.float32
F32R = mybir.dt.float32r
U32 = mybir.dt.uint32
ALU = mybir.AluOpType
ACT = mybir.ActivationFunctionType

SCW = T + P
C_COS = 0
C_SIN = C_COS + 2 * T
C_DEC = C_SIN + 2 * T
C_IDENT = C_DEC + HEADS * SCW
C_ONES = C_IDENT + P
C_CW = C_ONES + P
C_VEC = C_CW + DEPTH * KC * TAPS
VECS = ("mix", "convb", "lng", "lnb", "bga", "bgb", "bco", "ffn")
C_FIN = C_VEC + DEPTH * len(VECS) * KC
C_ROUT = C_FIN + KC
C_SM = C_ROUT + KC * NEXP
C_END = C_SM + 3 + NEXP


def build(nc, xt, wts, consts, out):
    with ExitStack() as ctx:
        def sem(name):
            return ctx.enter_context(nc.semaphore(name))

        base = [nc.sbuf_base + (-nc.sbuf_base) % 64]
        places = {}

        def sb(name, shape, dt=F32, over=None, skip=0):
            size = 4 * int(np.prod(shape[1:]))
            if over is None:
                at = base[0]
                base[0] += size + (-size) % 64
                places[name] = (at, size)
            else:
                at, room = places[over]
                at += skip
                assert skip + size <= room, name
            return nc.alloc_sbuf_tensor_at(name, shape, dt, offset=at)

        x = sb("x", [P, KC, T])
        hnh = sb("hnh", [P, KC, T], F32R)
        hnl = sb("hnl", [P, KC, T], F32R)
        raw = sb("raw", [P, RING, UNIT])
        whi = sb("whi", [P, RING, UNIT], F32R)
        wlo = sb("wlo", [P, RING, UNIT], F32R)
        con = sb("con", [P, C_END])
        q = sb("q", [P, HEADS, 2 * T])
        k = sb("k", [P, HEADS, 2 * T])
        uh = sb("uh", [P, KC, T], F32R, over="q")
        ul = sb("ul", [P, KC, T], F32R, over="k")
        v = sb("v", [P, HEADS, TT, VD])
        rl = sb("rl", [P, VC, T], F32R, over="v")
        g = sb("g", [P, VC, T])
        mh = sb("mh", [P, KC, T], F32R, over="g")
        ml = sb("ml", [P, KC, T], F32R, over="g", skip=4 * KC * T)
        prob = sb("prob", [P, HEADS, SCW])
        rsq = sb("rsq", [P, 2, 4, T])
        gated = sb("gated", [P, KC, T], F32, over="rsq")
        rh = sb("rh", [P, VC, T], F32R)
        xsq = sb("xsq", [P, KC, T], F32, over="rh")
        hn32 = sb("hn32", [P, KC, T], F32, over="rh", skip=4 * KC * T)
        sig = sb("sig", [P, 2, T], F32, over="rh")
        rot = sb("rot", [P, 2, 2, 2 * T], F32, over="rh", skip=8 * T)
        mga = sb("mga", [P, KC, T])
        mgb = sb("mgb", [P, KC, T])
        up = sb("up", [P, KC, PAD + T])
        lnsq = sb("lnsq", [P, KC, T], F32, over="up")
        cv = sb("cv", [P, KC, T])
        mtmp = sb("mtmp", [P, 2, T])
        diag = sb("diag", [P, HEADS, TT, P])
        small = sb("small", [P, 128])
        fs = sb("fs", [P, 2, T], F32, over="mga")
        f32_ = sb("f32_", [P, 2, T], F32, over="mga", skip=8 * T)
        fhh = sb("fhh", [P, 4, T], F32R, over="mgb")
        fhl = sb("fhl", [P, 4, T], F32R, over="mgb", skip=16 * T)
        gexp = sb("gexp", [P, NEXP, T], F32, over="g")
        edg = sb("edg", [P, 2, TT, P], F32, over="g", skip=4 * NEXP * T)
        yout = sb("yout", [P, KC, T], F32, over="cv")
        assert base[0] <= nc.sbuf_usable_end, base[0]

        pa = [ctx.enter_context(nc.psum_tensor(f"pa{i}", [P, 512], F32)) for i in range(4)]
        pb = [ctx.enter_context(nc.psum_tensor(f"pb{i}", [P, 512], F32)) for i in range(4)]

        cos2, sin2 = con[:, C_COS:C_COS + 2 * T], con[:, C_SIN:C_SIN + 2 * T]
        ident, ones = con[:, C_IDENT:C_IDENT + P], con[:, C_ONES:C_ONES + P]
        inv_d, inv_v, eps = (con[:, C_SM + i:C_SM + i + 1] for i in range(3))
        expert_no = con[:, C_SM + 3:C_SM + 3 + NEXP]

        def vec(l, what, c):
            at = C_VEC + (l * len(VECS) + VECS.index(what)) * KC + c
            return con[:, at:at + 1]

        def tap(l, c, t):
            at = C_CW + (l * KC + c) * TAPS + t
            return con[:, at:at + 1]

        landed = [sem(f"landed{i}") for i in range(RING)]
        con_in, x_in, out_done = sem("con_in"), sem("x_in"), sem("out_done")
        hi_done, lo_done, unit_done = sem("hi_done"), sem("lo_done"), sem("unit_done")
        pad_zero = sem("pad_zero")
        sq_done, stat_done, rms_done, inv_done = sem("sq_done"), sem("stat_done"), sem("rms_done"), sem("inv_done")
        dg_done, bc_done = sem("dg_done"), sem("bc_done")
        n32_done, nh_done, nl_done = sem("n32_done"), sem("nh_done"), sem("nl_done")
        x_done = sem("x_done")
        sig_done, u_done = sem("sig_done"), sem("u_done")
        rot_step, qk_done = sem("rot_step"), sem("qk_done")
        va_done, vb_done = sem("va_done"), sem("vb_done")
        score_done, prob_done = sem("score_done"), sem("prob_done")
        g_done, pv_done, rsq_done, rg_done = sem("g_done"), sem("pv_done"), sem("rsq_done"), sem("rg_done")
        rstat_done, rrms_done, rinv_done, rdg_done, rbc_done = (sem(n) for n in (
            "rstat_done", "rrms_done", "rinv_done", "rdg_done", "rbc_done"))
        rn_done, rh_done, rl_done = sem("rn_done"), sem("rh_done"), sem("rl_done")
        mg_done = sem("mg_done")
        conv = sem("conv")
        lmean, lmeans, lmdg, lmbc, lcen = (sem(n) for n in ("lmean", "lmeans", "lmdg", "lmbc", "lcen"))
        lsq, lstat, lrms, linv, ldg, lbc, lnrm = (sem(n) for n in (
            "lsq", "lstat", "lrms", "linv", "ldg", "lbc", "lnrm"))
        lact, uh_done, ul_done = sem("lact"), sem("uh_done"), sem("ul_done")
        gated_done, mstep, mh_done, ml_done = sem("gated_done"), sem("mstep"), sem("mh_done"), sem("ml_done")
        fs_done, f32_done, fh_done, fl_done = sem("fs_done"), sem("f32_done"), sem("fh_done"), sem("fl_done")
        logit_done, top, ex_done = sem("logit_done"), sem("top"), sem("ex_done")
        edg_done, ebc_done, gexp_done = sem("edg_done"), sem("ebc_done"), sem("gexp_done")
        fin_done = sem("fin_done")

        block = ctx.enter_context(nc.Block())

        FF0 = (0, DENSE_CHUNKS)

        @block.sync
        def _(sp):
            sp.dma_start(con[:, :], consts).then_inc(con_in, 16)

            def load(u, slot):
                sp.dma_start(raw[:, slot, :], wts[u]).then_inc(landed[slot], 16)
            for s in range(RING):
                load(s, s)
            n = UNITS // RING - 1
            with sp.Fori(0, n, 1) as it:
                for s in range(RING):
                    sp.wait_ge(lo_done, it * RING + (s + 1))
                    load(bass.ds(it * RING + (RING + s), 1), s)
            for s in range(UNITS % RING):
                sp.wait_ge(lo_done, n * RING + s + 1)
                load((n + 1) * RING + s, s)
            sp.wait_ge(fin_done, 4)
            sp.dma_start(out, yout[:, :, :]).then_inc(out_done, 16)
            sp.wait_ge(out_done, 16)

        @block.gpsimd
        def _(pool):
            nc.gpsimd.memset(up[:, :, 0:PAD], 0.0).then_inc(pad_zero, 1)
            pool.wait_ge(lact, KC)
            nc.gpsimd.memset(up[:, :, 0:PAD], 0.0).then_inc(pad_zero, 1)

        @block.scalar
        def _(act):
            act.dma_start(x[:, :, :], xt).then_inc(x_in, 16)

            def split_hi(u):
                if isinstance(u, int) and u >= UNITS:
                    return
                act.wait_ge(landed[u % RING], 16 * (u // RING + 1))
                if u >= RING:
                    act.wait_ge(unit_done, u - RING + 1)
                nc.scalar.copy(whi[:, u % RING, :], raw[:, u % RING, :]).then_inc(hi_done, 1)

            def norm(n):
                for c in range(4):
                    if n == 0:
                        act.wait_ge(x_in, 16)
                    else:
                        act.wait_ge(x_done, 4 * (n - 1) + c + 1)
                    nc.scalar.activation(xsq[:, 2 * c:2 * c + 2, :], x[:, 2 * c:2 * c + 2, :],
                                         ACT.Square).then_inc(sq_done, 1)
                act.wait_ge(stat_done, n + 1)
                if n == 0:
                    act.wait_ge(con_in, 16)
                nc.scalar.activation(small[:, 0:TT], pb[2][:, 0:TT], ACT.Sqrt, bias=eps).then_inc(rms_done, 1)
                if n == 2 * DEPTH:
                    return
                for c in range(4):
                    act.wait_ge(n32_done, 8 * n + 2 * c + 2)
                    nc.scalar.copy(hnh[:, 2 * c:2 * c + 2, :], hn32[:, 2 * c:2 * c + 2, :]).then_inc(nh_done, 1)

            def mixer(l):
                U = LAYER0[l]
                for p in range(8):
                    split_hi(U + GLU0 + 2 * p + 4)
                    act.wait_ge(unit_done, U + GLU0 + 2 * p + 2)
                    if 8 * l + p >= 2:
                        act.wait_ge(u_done, 8 * l + p - 1)
                    nc.scalar.activation(sig[:, p % 2, :], pa[p % 4][:, T:2 * T], ACT.Sigmoid).then_inc(sig_done, 1)
                    split_hi(U + GLU0 + 2 * p + 5)
                for j in range(N_QK):
                    split_hi(U + QK0 + j + 4)
                for cg in range(4):
                    for j in range(3):
                        split_hi(U + V0 + 4 * cg + j + 4)
                    act.wait_ge(unit_done, U + V0 + 4 * cg + 4)
                    nc.scalar.copy(v[:, cg, 0, :], pa[(2 * cg) % 4][:, :]).then_inc(va_done, 1)
                    split_hi(U + V0 + 4 * cg + 7)
                def squares(h):
                    act.wait_ge(pv_done, 4 * l + h + 1)
                    if 4 * l + h >= 2:
                        act.wait_ge(rstat_done, 4 * l + h - 1)
                    for b in range(2):
                        nc.scalar.activation(rsq[:, h % 2, 2 * b:2 * b + 2, :], pb[b][:, :],
                                             ACT.Square).then_inc(rsq_done, 1)
                for p in range(8):
                    split_hi(U + G0 + 2 * p + 4)
                    act.wait_ge(unit_done, U + G0 + 2 * p + 2)
                    nc.scalar.activation(g[:, 2 * p:2 * p + 2, :], pa[p % 4][:, :], ACT.Silu).then_inc(g_done, 1)
                    split_hi(U + G0 + 2 * p + 5)
                    if p in (3, 5, 7):
                        squares((p - 3) // 2)
                for p in range(8):
                    split_hi(U + MG0 + 2 * p + 4)
                    act.wait_ge(unit_done, U + MG0 + 2 * p + 2)
                    nc.scalar.activation(mga[:, p, :], pa[p % 4][:, 0:T], ACT.Sigmoid, bias=vec(l, "bga", p))
                    nc.scalar.activation(mgb[:, p, :], pa[p % 4][:, T:2 * T], ACT.Sigmoid,
                                         bias=vec(l, "bgb", p)).then_inc(mg_done, 1)
                    split_hi(U + MG0 + 2 * p + 5)
                    if p == 0:
                        squares(3)
                    if p == 2:
                        act.wait_ge(rstat_done, 4 * l + 4)
                        nc.scalar.activation(small[:, 8:16], pb[2][:, 8:16], ACT.Sqrt, bias=eps).then_inc(rrms_done, 1)
                    if p >= 4:
                        h = p - 4
                        act.wait_ge(rn_done, 4 * l + h + 1)
                        nc.scalar.copy(rh[:, 4 * h:4 * h + 4, :], g[:, 4 * h:4 * h + 4, :]).then_inc(rh_done, 1)
                for j in range(N_RO):
                    split_hi(U + RO0 + j + 4)
                    if j == 2:
                        act.wait_ge(lmean, l + 1)
                        nc.scalar.copy(small[:, 32:34], pb[2][:, 32:34]).then_inc(lmeans, 1)
                    if 6 <= j < 10:
                        c = j - 6
                        act.wait_ge(lcen, 8 * l + 2 * c + 2)
                        nc.scalar.activation(lnsq[:, 2 * c:2 * c + 2, :], cv[:, 2 * c:2 * c + 2, :],
                                             ACT.Square).then_inc(lsq, 1)
                    if j == 11:
                        act.wait_ge(lstat, l + 1)
                        nc.scalar.activation(small[:, 36:38], pb[2][:, 36:38], ACT.Sqrt, bias=eps).then_inc(lrms, 1)
                    if j >= 14:
                        for c in range(4 * (j - 14), 4 * (j - 14) + 4):
                            act.wait_ge(lnrm, 8 * l + c + 1)
                            nc.scalar.activation(cv[:, c, :], cv[:, c, :], ACT.Silu, bias=vec(l, "lnb", c),
                                                 scale=vec(l, "lng", c)).then_inc(lact, 1)
                        for c in range(2 * (j - 14), 2 * (j - 14) + 2):
                            act.wait_ge(lact, 8 * l + 2 * c + 2)
                            nc.scalar.copy(uh[:, 2 * c:2 * c + 2, :], cv[:, 2 * c:2 * c + 2, :]).then_inc(uh_done, 1)
                for j in range(N_CO):
                    split_hi(U + CO0 + j + 4)
                    if j >= 1:
                        c = j - 1
                        act.wait_ge(mstep, 3 * (8 * l + c) + 3)
                        nc.scalar.copy(mh[:, c, :], cv[:, c, :]).then_inc(mh_done, 1)
                act.wait_ge(mstep, 3 * (8 * l + 7) + 3)
                nc.scalar.copy(mh[:, 7, :], cv[:, 7, :]).then_inc(mh_done, 1)
                for j in range(N_WO):
                    split_hi(U + WO0 + j + 4)

            def ffn(l):
                U = LAYER0[l] + MIXER_UNITS
                F = FFN_CHUNKS[l]
                f0 = FF0[l]
                if l == 1:
                    act.wait_ge(top, 4)
                    nc.scalar.activation(small[:, 80:80 + TT], small[:, 76:76 + TT], ACT.Exp).then_inc(ex_done, 1)
                for f in range(F):
                    if f:
                        split_hi(U + 3 * f + 3)
                    act.wait_ge(unit_done, U + 3 * f + 1 + (f == 0))
                    if f0 + f >= 2:
                        act.wait_ge(f32_done, f0 + f - 1)
                    nc.scalar.activation(fs[:, f % 2, :], pa[f % 4][:, 0:T], ACT.Silu).then_inc(fs_done, 1)
                    split_hi(U + 3 * f + 4)
                    act.wait_ge(f32_done, f0 + f + 1)
                    if f >= 4:
                        act.wait_ge(unit_done, U + 3 * (f - 4) + 5)
                    nc.scalar.copy(fhh[:, f % 4, :], f32_[:, f % 2, :]).then_inc(fh_done, 1)
                    split_hi(U + 3 * f + 5)
                split_hi(U + 3 * F + 3)

            for s in range(4):
                split_hi(s)
            norm(0)
            for l in range(DEPTH):
                mixer(l)
                norm(2 * l + 1)
                ffn(l)
                norm(2 * l + 2)

        @block.vector
        def _(dve):
            def split_lo(u):
                if u >= UNITS:
                    return
                dve.wait_ge(hi_done, u + 1)
                if u >= RING:
                    dve.wait_ge(unit_done, u - RING + 1)
                nc.vector.tensor_tensor(wlo[:, u % RING, :], raw[:, u % RING, :],
                                        whi[:, u % RING, :].bitcast(F32), ALU.subtract).then_inc(lo_done, 1)

            def conv_ops(l, first, last):
                for n in range(first, min(last, KC * TAPS)):
                    c, t = 2 * (n // (2 * TAPS)) + n % 2, (n % (2 * TAPS)) // 2
                    if t == 0:
                        if n % 2 == 0:
                            dve.wait_ge(u_done, 8 * l + c + 2)
                        nc.vector.tensor_scalar(cv[:, c, :], up[:, c, 0:T], tap(l, c, 0), vec(l, "convb", c),
                                                ALU.mult, ALU.add).then_inc(conv, 1)
                        continue
                    dve.wait_ge(conv, l * KC * TAPS + n - 1)
                    nc.vector.scalar_tensor_tensor(out=cv[:, c, :], in0=up[:, c, t:t + T], scalar=tap(l, c, t),
                                                   in1=cv[:, c, :], op0=ALU.mult, op1=ALU.add).then_inc(conv, 1)

            def norm(n):
                dve.wait_ge(rms_done, n + 1)
                nc.vector.reciprocal(small[:, 4:4 + TT], small[:, 0:TT]).then_inc(inv_done, 1)
                dve.wait_ge(inv_done, n + 1)
                for t in range(TT):
                    nc.vector.tensor_scalar(diag[:, 0, t, :], ident, small[:, 4 + t:5 + t], None,
                                            ALU.mult).then_inc(dg_done, 1)
                dve.wait_ge(bc_done, n + 1)
                last = n == 2 * DEPTH
                for c in range(KC):
                    gain = con[:, C_FIN + c:C_FIN + c + 1] if last else vec(n // 2, ("mix", "ffn")[n % 2], c)
                    nc.vector.scalar_tensor_tensor(out=(yout if last else hn32)[:, c, :], in0=x[:, c, :], scalar=gain,
                                                   in1=pb[3][:, 0:T], op0=ALU.mult, op1=ALU.mult).then_inc(
                                                       fin_done if last and c % 2 else n32_done, 1)
                if last:
                    return
                for c in range(4):
                    dve.wait_ge(nh_done, 4 * n + c + 1)
                    nc.vector.tensor_tensor(hnl[:, 2 * c:2 * c + 2, :], hn32[:, 2 * c:2 * c + 2, :],
                                            hnh[:, 2 * c:2 * c + 2, :].bitcast(F32), ALU.subtract).then_inc(nl_done, 1)

            def mixer(l):
                U = LAYER0[l]
                for p in range(8):
                    split_lo(U + GLU0 + 2 * p + 4)
                    dve.wait_ge(sig_done, 8 * l + p + 1)
                    if p == 0:
                        dve.wait_ge(pad_zero, l + 1)
                    nc.vector.tensor_tensor(up[:, p, PAD:], pa[p % 4][:, 0:T], sig[:, p % 2, :],
                                            ALU.mult).then_inc(u_done, 1)
                    split_lo(U + GLU0 + 2 * p + 5)
                    conv_ops(l, 6 * max(0, p - 3), 6 * max(0, p - 2))
                done = 30
                for p in range(8):
                    dst, h = (q, p) if p < 4 else (k, p - 4)
                    split_lo(U + QK0 + 2 * p + 4)
                    dve.wait_ge(unit_done, U + QK0 + 2 * p + 2)
                    if p >= 2 or l:
                        dve.wait_ge(qk_done, 2 * (8 * l + p - 1))
                    nc.vector.tensor_tensor(rot[:, p % 2, 0, :], pa[p % 4][:, :], cos2, ALU.mult).then_inc(rot_step, 1)
                    nc.vector.tensor_tensor(rot[:, p % 2, 1, :], pa[p % 4][:, :], sin2, ALU.mult).then_inc(rot_step, 1)
                    conv_ops(l, done, done + 2)
                    split_lo(U + QK0 + 2 * p + 5)
                    dve.wait_ge(rot_step, 2 * (8 * l + p + 1))
                    nc.vector.tensor_tensor(dst[:, h, 0:T], rot[:, p % 2, 0, 0:T], rot[:, p % 2, 1, T:],
                                            ALU.subtract).then_inc(qk_done, 1)
                    nc.vector.tensor_tensor(dst[:, h, T:], rot[:, p % 2, 1, 0:T], rot[:, p % 2, 0, T:],
                                            ALU.add).then_inc(qk_done, 1)
                    done += 2
                for cg in range(4):
                    for j in range(3):
                        split_lo(U + V0 + 4 * cg + j + 4)
                        conv_ops(l, done, done + 4)
                        done += 4
                    dve.wait_ge(unit_done, U + V0 + 4 * cg + 4)
                    nc.vector.tensor_copy(v[:, cg, 1, :], pa[(2 * cg + 1) % 4][:, :]).then_inc(vb_done, 1)
                    split_lo(U + V0 + 4 * cg + 7)
                    conv_ops(l, done, done + 3)
                    done += 3
                for h in range(HEADS):
                    dve.wait_ge(score_done, 4 * l + h + 1)
                    nc.vector.tensor_tensor(prob[:, h, :], pb[h][:, 0:SCW], con[:, C_DEC + h * SCW:C_DEC + (h + 1) * SCW],
                                            ALU.mult).then_inc(prob_done, 1)
                conv_ops(l, done, done + 6)
                done += 6

                def gate_r(h):
                    dve.wait_ge(pv_done, 4 * l + h + 1)
                    dve.wait_ge(g_done, 8 * l + 2 * h + 2)
                    for b in range(2):
                        c = 4 * h + 2 * b
                        dve.wait_ge(rsq_done, 8 * l + 2 * h + b + 1)
                        nc.vector.tensor_tensor(g[:, c:c + 2, :], pb[b][:, :].rearrange("p (c t) -> p c t", c=2),
                                                g[:, c:c + 2, :], ALU.mult).then_inc(rg_done, 1)
                for p in range(8):
                    split_lo(U + G0 + 2 * p + 4)
                    conv_ops(l, done, done + 5)
                    done += 5
                    split_lo(U + G0 + 2 * p + 5)
                    conv_ops(l, done, done + 4)
                    done += 4
                    if p in (3, 5, 7):
                        gate_r((p - 3) // 2)
                for p in range(8):
                    split_lo(U + MG0 + 2 * p + 4)
                    if p == 0:
                        gate_r(3)
                    if p == 2:
                        dve.wait_ge(rrms_done, l + 1)
                        nc.vector.reciprocal(small[:, 16:24], small[:, 8:16]).then_inc(rinv_done, 1)
                        dve.wait_ge(rinv_done, l + 1)
                        for h in range(HEADS):
                            for t in range(TT):
                                nc.vector.tensor_scalar(diag[:, h, t, :], ident, small[:, 16 + 2 * h + t:17 + 2 * h + t],
                                                        None, ALU.mult).then_inc(rdg_done, 1)
                    if p >= 4:
                        h = p - 4
                        dve.wait_ge(rbc_done, 4 * l + 4)
                        bc = pb[h // 2][:, (h % 2) * T:(h % 2) * T + T]
                        nc.vector.tensor_tensor(g[:, 4 * h:4 * h + 4, :], g[:, 4 * h:4 * h + 4, :],
                                                bc.rearrange("p (o t) -> p o t", o=1).broadcast_to([P, 4, T]),
                                                ALU.mult).then_inc(rn_done, 1)
                    conv_ops(l, done, done + 4)
                    done += 4
                    split_lo(U + MG0 + 2 * p + 5)
                    conv_ops(l, done, done + 3)
                    done += 3
                    if p >= 4:
                        dve.wait_ge(rh_done, 4 * l + h + 1)
                        nc.vector.tensor_tensor(rl[:, 4 * h:4 * h + 4, :], g[:, 4 * h:4 * h + 4, :],
                                                rh[:, 4 * h:4 * h + 4, :].bitcast(F32), ALU.subtract).then_inc(rl_done, 1)
                conv_ops(l, done, KC * TAPS)
                for j in range(N_RO):
                    split_lo(U + RO0 + j + 4)
                    if j % 2 == 1:
                        c = j // 2
                        dve.wait_ge(unit_done, U + RO0 + j + 1)
                        if c == 0:
                            dve.wait_ge(mg_done, 8 * l + 8)
                        nc.vector.tensor_tensor(gated[:, c, :], pa[c % 4][:, 0:T],
                                                mga[:, c, :], ALU.mult).then_inc(gated_done, 1)
                    if j == 3:
                        dve.wait_ge(lmeans, l + 1)
                        for t in range(TT):
                            nc.vector.tensor_scalar(diag[:, 0, t, :], ident, small[:, 32 + t:33 + t], None,
                                                    ALU.mult).then_inc(lmdg, 1)
                    if j == 5:
                        dve.wait_ge(lmbc, l + 1)
                        for c in range(KC):
                            nc.vector.tensor_tensor(cv[:, c, :], cv[:, c, :], pb[3][:, 0:T], ALU.subtract).then_inc(lcen, 1)
                    if j == 11:
                        dve.wait_ge(lrms, l + 1)
                        nc.vector.reciprocal(small[:, 40:42], small[:, 36:38]).then_inc(linv, 1)
                        dve.wait_ge(linv, l + 1)
                        for t in range(TT):
                            nc.vector.tensor_scalar(diag[:, 1, t, :], ident, small[:, 40 + t:41 + t], None,
                                                    ALU.mult).then_inc(ldg, 1)
                    if j == 13:
                        dve.wait_ge(lbc, l + 1)
                        for c in range(KC):
                            nc.vector.tensor_tensor(cv[:, c, :], cv[:, c, :], pb[3][:, T:2 * T], ALU.mult).then_inc(lnrm, 1)
                    if j >= 14:
                        for c in range(2 * (j - 14), 2 * (j - 14) + 2):
                            dve.wait_ge(uh_done, 4 * l + c + 1)
                            nc.vector.tensor_tensor(ul[:, 2 * c:2 * c + 2, :], cv[:, 2 * c:2 * c + 2, :],
                                                    uh[:, 2 * c:2 * c + 2, :].bitcast(F32), ALU.subtract).then_inc(ul_done, 1)

                def merged_lo(c):
                    dve.wait_ge(mh_done, 8 * l + c + 1)
                    nc.vector.tensor_tensor(ml[:, c, :], cv[:, c, :], mh[:, c, :].bitcast(F32),
                                            ALU.subtract).then_inc(ml_done, 1)
                for c in range(N_CO):
                    n = 3 * (8 * l + c)
                    dve.wait_ge(unit_done, U + CO0 + c + 1)
                    nc.vector.scalar_tensor_tensor(out=mtmp[:, c % 2, :], in0=pa[c % 4][:, 0:T],
                                                   scalar=vec(l, "bco", c), in1=mgb[:, c, :], op0=ALU.add,
                                                   op1=ALU.mult).then_inc(mstep, 1)
                    dve.wait_ge(ul_done, 4 * l + 4)
                    dve.wait_ge(mstep, n + 1)
                    nc.vector.tensor_tensor(cv[:, c, :], mtmp[:, c % 2, :], gated[:, c, :], ALU.add).then_inc(mstep, 2)
                    split_lo(U + CO0 + c + 4)
                    if c >= 1:
                        merged_lo(c - 1)
                merged_lo(7)
                for p in range(4):
                    split_lo(U + WO0 + 2 * p + 4)
                    dve.wait_ge(unit_done, U + WO0 + 2 * p + 2)
                    xx = x[:, 2 * p:2 * p + 2, :]
                    nc.vector.tensor_tensor(xx, pa[p % 4][:, :].rearrange("p (c t) -> p c t", c=2), xx,
                                            ALU.add).then_inc(x_done, 1)
                    split_lo(U + WO0 + 2 * p + 5)

            def route():
                lg, mx, ix = small[:, 48:64], small[:, 84:100], small[:, 100:116].bitcast(U32)
                dve.wait_ge(logit_done, 1)
                nc.vector.tensor_copy(lg, pb[2][:, 48:64]).then_inc(top, 1)
                dve.wait_ge(top, 1)
                for t in range(TT):
                    nc.vector.max(mx[:, 8 * t:8 * t + 8], lg[:, 8 * t:8 * t + 8]).then_inc(top, 1)
                dve.wait_ge(top, 3)
                m = mx.rearrange("p (t e) -> p t e", t=TT)
                nc.vector.tensor_tensor(small[:, 76:78].rearrange("p (t o) -> p t o", o=1), m[:, :, 1:2], m[:, :, 0:1],
                                        ALU.subtract).then_inc(top, 1)
                for t in range(TT):
                    nc.vector.max_index(ix[:, 8 * t:8 * t + 8], mx[:, 8 * t:8 * t + 8],
                                        lg[:, 8 * t:8 * t + 8]).then_inc(top, 1)
                dve.wait_ge(top, 6)
                ixf = small[:, 116:120]
                nc.vector.tensor_copy(ixf.rearrange("p (k t) -> p t k", k=2),
                                      ix.rearrange("p (t e) -> p t e", t=TT)[:, :, 0:2]).then_inc(top, 1)
                dve.wait_ge(ex_done, 1)
                e = small[:, 80:80 + TT]
                nc.vector.tensor_scalar(small[:, 82:84], e, 1.0, None, ALU.add).then_inc(top, 1)
                dve.wait_ge(top, 8)
                wt = small[:, 120:124]
                nc.vector.reciprocal(wt[:, 0:2], small[:, 82:84]).then_inc(top, 1)
                dve.wait_ge(top, 9)
                nc.vector.tensor_tensor(wt[:, 2:4], wt[:, 0:2], e, ALU.mult).then_inc(top, 1)
                dve.wait_ge(top, 10)
                gt = small[:, 48:64]
                g2 = small[:, 84:100]
                for t in range(TT):
                    nc.vector.tensor_scalar(gt[:, 8 * t:8 * t + 8], expert_no, ixf[:, t:t + 1], wt[:, t:t + 1],
                                            ALU.is_equal, ALU.mult).then_inc(top, 1)
                    nc.vector.tensor_scalar(g2[:, 8 * t:8 * t + 8], expert_no, ixf[:, 2 + t:3 + t], wt[:, 2 + t:3 + t],
                                            ALU.is_equal, ALU.mult).then_inc(top, 1)
                dve.wait_ge(top, 14)
                nc.vector.tensor_tensor(gt, gt, g2, ALU.add).then_inc(top, 1)
                dve.wait_ge(top, 15)
                for ex in range(NEXP):
                    if ex >= 2:
                        dve.wait_ge(ebc_done, ex - 1)
                    for t in range(TT):
                        nc.vector.tensor_scalar(edg[:, ex % 2, t, :], ident, gt[:, 8 * t + ex:8 * t + ex + 1], None,
                                                ALU.mult).then_inc(edg_done, 1)
                    dve.wait_ge(ebc_done, ex + 1)
                    nc.vector.tensor_copy(gexp[:, ex, :], pb[ex % 2][:, 0:T]).then_inc(gexp_done, 1)

            def ffn(l):
                U = LAYER0[l] + MIXER_UNITS
                F = FFN_CHUNKS[l]
                f0 = FF0[l]
                if l == 1:
                    route()
                for f in range(F):
                    if f:
                        split_lo(U + 3 * f + 3)
                    dve.wait_ge(fs_done, f0 + f + 1)
                    nc.vector.tensor_tensor(f32_[:, f % 2, :], fs[:, f % 2, :], pa[f % 4][:, T:2 * T],
                                            ALU.mult).then_inc(f32_done if l == 0 else top, 1)
                    if l == 1:
                        dve.wait_ge(top, 16 + f)
                        nc.vector.tensor_tensor(f32_[:, f % 2, :], f32_[:, f % 2, :], gexp[:, f // EXP_CHUNKS, :],
                                                ALU.mult).then_inc(f32_done, 1)
                    split_lo(U + 3 * f + 4)
                    dve.wait_ge(fh_done, f0 + f + 1)
                    nc.vector.tensor_tensor(fhl[:, f % 4, :], f32_[:, f % 2, :], fhh[:, f % 4, :].bitcast(F32),
                                            ALU.subtract).then_inc(fl_done, 1)
                    split_lo(U + 3 * f + 5)
                split_lo(U + 3 * F + 3)
                dve.wait_ge(unit_done, U + 3 * F)
                for p in range(4):
                    xx = x[:, 2 * p:2 * p + 2, :]
                    nc.vector.tensor_tensor(xx, pb[p][:, :].rearrange("p (c t) -> p c t", c=2), xx,
                                            ALU.add).then_inc(x_done, 1)

            dve.wait_ge(con_in, 16)
            dve.wait_ge(x_in, 16)
            for s in range(4):
                split_lo(s)
            norm(0)
            for l in range(DEPTH):
                mixer(l)
                norm(2 * l + 1)
                ffn(l)
                norm(2 * l + 2)

        @block.tensor
        def _(pe):
            mm = nc.tensor.matmul

            def tiles(u, dst, xh, xl, kind="m", first=True, last=True):
                s = u % RING
                pe.wait_ge(hi_done, u + 1)
                for i in range(8):
                    w = whi[:, s, i * P:(i + 1) * P]
                    mm(dst(i), w, xh(i), start=first(i), stop=False, skip_group_check=True)
                    mm(dst(i), w, xl(i), start=False, stop=False, skip_group_check=True)
                pe.wait_ge(lo_done, u + 1)
                for i in range(8):
                    ins = mm(dst(i), wlo[:, s, i * P:(i + 1) * P], xh(i), start=False, stop=last(i),
                             skip_group_check=True)
                ins.then_inc(unit_done, 1)

            def project(u, dst, ah, al, k0=0, first=True, last=True):
                tiles(u, lambda i: dst, lambda i: ah[:, k0 + i, :], lambda i: al[:, k0 + i, :],
                      first=lambda i: first and i == 0, last=lambda i: last and i == 7)

            def stat(dst, src, cols, scale, done):
                for t in range(TT):
                    for i, c in enumerate(cols):
                        ins = mm(dst[:, t:t + 1], src(c)[:, t * P:(t + 1) * P], scale, start=i == 0,
                                 stop=i == len(cols) - 1)
                ins.then_inc(done, 1)

            def spread(dst, d, done):
                mm(dst, ones, d.rearrange("p t n -> p (t n)"), start=True, stop=True).then_inc(done, 1)

            def norm(n):
                if n == 0:
                    pe.wait_ge(con_in, 16)
                elif n % 2 == 0:
                    pe.wait_ge(x_done, 4 * n)
                for t in range(TT):
                    for c in range(KC):
                        if t == 0 and c % 2 == 0:
                            pe.wait_ge(sq_done, 4 * n + c // 2 + 1)
                        ins = mm(pb[2][:, t:t + 1], xsq[:, c, t * P:(t + 1) * P], inv_d, start=c == 0, stop=c == KC - 1)
                ins.then_inc(stat_done, 1)
                pe.wait_ge(dg_done, 2 * n + 2)
                spread(pb[3][:, 0:T], diag[:, 0, :, :], bc_done)
                if n < 2 * DEPTH:
                    if n == 3:
                        pe.wait_ge(n32_done, 8 * n + 8)
                        for t in range(TT):
                            for c in range(KC):
                                ins = mm(pb[2][:, 48 + 8 * t:56 + 8 * t], hn32[:, c, t * P:(t + 1) * P],
                                         con[:, C_ROUT + c * NEXP:C_ROUT + (c + 1) * NEXP],
                                         start=c == 0, stop=c == KC - 1)
                        ins.then_inc(logit_done, 1)
                        for ex in range(NEXP):
                            pe.wait_ge(edg_done, 2 * ex + 2)
                            if ex >= 2:
                                pe.wait_ge(gexp_done, ex - 1)
                            spread(pb[ex % 2][:, 0:T], edg[:, ex % 2, :, :], ebc_done)
                        pe.wait_ge(gexp_done, NEXP)
                    pe.wait_ge(nh_done, 4 * n + 4)
                    pe.wait_ge(nl_done, 4 * n + 4)

            def mixer(l):
                U = LAYER0[l]

                def half(j):
                    return pa[(j // 2) % 4][:, (j % 2) * T:(j % 2) * T + T]

                for j in range(N_GLU):
                    project(U + GLU0 + j, half(j), hnh, hnl)
                for j in range(N_QK):
                    project(U + QK0 + j, half(j), hnh, hnl)
                for cg in range(4):
                    for j in range(4):
                        u = U + V0 + 4 * cg + j
                        s = u % RING
                        pe.wait_ge(hi_done, u + 1)
                        for part in range(2):
                            if part:
                                pe.wait_ge(lo_done, u + 1)
                            for kk in range(2):
                                w = (wlo if part else whi)[:, s, kk * 512:(kk + 1) * 512]
                                for t in range(TT):
                                    dst = pa[(2 * cg + t) % 4][:, :]
                                    for a in ((hnh,) if part else (hnh, hnl)):
                                        ins = mm(dst, a[:, 2 * j + kk, t * P:(t + 1) * P], w,
                                                 start=j == 0 and kk == 0 and part == 0 and a is hnh,
                                                 stop=j == 3 and part == 1 and kk == 1, skip_group_check=True)
                        ins.then_inc(unit_done, 1)
                pe.wait_ge(qk_done, 16 * l + 16)
                for h in range(HEADS):
                    for t in range(TT):
                        n0, dst = t * P, pb[h][:, 0:T] if t == 0 else pb[h][:, T:SCW]
                        for c in range(2):
                            ins = mm(dst, k[:, h, c * T + t * P:c * T + (t + 1) * P], q[:, h, c * T + n0:(c + 1) * T],
                                     start=c == 0, stop=c == 1)
                    ins.then_inc(score_done, 1)

                def pv(h):
                    pe.wait_ge(prob_done, 4 * l + 4)
                    pe.wait_ge(va_done, 4 * l + h + 1)
                    pe.wait_ge(vb_done, 4 * l + h + 1)
                    if h:
                        pe.wait_ge(rg_done, 8 * l + 2 * h)
                        pe.wait_ge(rsq_done, 8 * l + 2 * h)
                    for e in range(4):
                        dst = pb[e // 2]
                        o = (e % 2) * T
                        mm(dst[:, o:o + T], v[:, h, 0, e * P:(e + 1) * P], prob[:, h, 0:T], start=True, stop=True)
                        ins = mm(dst[:, o + P:o + T], v[:, h, 1, e * P:(e + 1) * P], prob[:, h, T:SCW], start=False,
                                 stop=True, skip_group_check=True)
                    ins.then_inc(pv_done, 1)

                def rstat(h):
                    pe.wait_ge(rsq_done, 8 * l + 2 * h + 2)
                    stat(pb[2][:, 8 + 2 * h:10 + 2 * h], lambda c: rsq[:, h % 2, c, :], range(4), inv_v, rstat_done)
                for p in range(8):
                    project(U + G0 + 2 * p, half(2 * p), hnh, hnl)
                    project(U + G0 + 2 * p + 1, half(2 * p + 1), hnh, hnl)
                    if p in (2, 4, 6):
                        pv((p - 2) // 2)
                    if p in (5, 7):
                        rstat((p - 5) // 2)
                for p in range(8):
                    project(U + MG0 + 2 * p, half(2 * p), hnh, hnl)
                    project(U + MG0 + 2 * p + 1, half(2 * p + 1), hnh, hnl)
                    if p == 0:
                        rstat(2)
                        pv(3)
                    if p == 1:
                        rstat(3)
                    if p == 3:
                        for h in range(HEADS):
                            if h == 0:
                                pe.wait_ge(rg_done, 8 * l + 8)
                                pe.wait_ge(rsq_done, 8 * l + 8)
                            pe.wait_ge(rdg_done, 8 * l + 2 * h + 2)
                            spread(pb[h // 2][:, (h % 2) * T:(h % 2) * T + T], diag[:, h, :, :], rbc_done)
                pe.wait_ge(rh_done, 4 * l + 4)
                pe.wait_ge(rl_done, 4 * l + 4)
                for j in range(N_RO):
                    c = j // 2
                    project(U + RO0 + j, pa[c % 4][:, 0:T], rh, rl, k0=8 * (j % 2), first=j % 2 == 0, last=j % 2 == 1)
                    if j == 1:
                        pe.wait_ge(conv, (l + 1) * KC * TAPS)
                        stat(pb[2][:, 32:34], lambda c: cv[:, c, :], range(KC), inv_d, lmean)
                    if j == 4:
                        pe.wait_ge(lmdg, 2 * l + 2)
                        spread(pb[3][:, 0:T], diag[:, 0, :, :], lmbc)
                    if j == 10:
                        pe.wait_ge(lsq, 4 * l + 4)
                        stat(pb[2][:, 36:38], lambda c: lnsq[:, c, :], range(KC), inv_d, lstat)
                    if j == 12:
                        pe.wait_ge(ldg, 2 * l + 2)
                        spread(pb[3][:, T:2 * T], diag[:, 1, :, :], lbc)
                pe.wait_ge(uh_done, 4 * l + 4)
                pe.wait_ge(ul_done, 4 * l + 4)
                for j in range(N_CO):
                    if j >= 4:
                        pe.wait_ge(mstep, 3 * (8 * l + j - 4) + 1)
                    project(U + CO0 + j, pa[j % 4][:, 0:T], uh, ul)
                pe.wait_ge(mh_done, 8 * l + 8)
                pe.wait_ge(ml_done, 8 * l + 8)
                for j in range(N_WO):
                    project(U + WO0 + j, half(j), mh, ml)

            def ffn(l):
                U = LAYER0[l] + MIXER_UNITS
                F = FFN_CHUNKS[l]
                f0 = FF0[l]

                def down(f, u):
                    pe.wait_ge(fh_done, f0 + f + 1)
                    pe.wait_ge(fl_done, f0 + f + 1)
                    tiles(u, lambda i: pb[i // 2][:, (i % 2) * T:(i % 2) * T + T], lambda i: fhh[:, f % 4, :],
                          lambda i: fhl[:, f % 4, :], first=lambda i: f == 0 and i % 2 == 0,
                          last=lambda i: f == F - 1)
                for f in range(F + 1):
                    if f < F:
                        u = U + 3 * f - (f > 0)
                        project(u, pa[f % 4][:, 0:T], hnh, hnl)
                        project(u + 1, pa[f % 4][:, T:2 * T], hnh, hnl)
                    if f:
                        down(f - 1, U + 3 * f + 1 - (f == F) * 2)

            norm(0)
            for l in range(DEPTH):
                mixer(l)
                norm(2 * l + 1)
                ffn(l)
                norm(2 * l + 2)


def columns(w):
    kk, n = w.shape
    w = w.reshape(kk // D, KC, P, n // P, P)
    return w.transpose(3, 0, 2, 1, 4).reshape(-1, P, UNIT)


def wide(w):
    w = w.reshape(4, 2, P, w.shape[1] // 512, 512)
    return w.transpose(3, 0, 2, 1, 4).reshape(-1, P, UNIT)


def ffn_units(w1, w3, w2):
    a, b, c = columns(w1), columns(w3), w2.reshape(-1, P, UNIT)
    return a, b, c


def kernel(**inputs):
    import concourse.bacc as bacc
    from concourse.bass_utils import run_bass_kernel_spmd as run

    a = {n: np.asarray(v) for n, v in inputs.items()}

    def pairs(u, w):
        return np.stack([u, w], 1).reshape(-1, P, UNIT)

    wts = np.empty((UNITS, P, UNIT), np.float32)
    for l in range(DEPTH):
        U = LAYER0[l]
        w_in = a["w_in"][l]
        cut = np.cumsum([0, D, D, VW, VW, D, D, D, D])
        wq, wk, wv, wg, wval, wgate, wga, wgb = (w_in[:, cut[i]:cut[i + 1]] for i in range(8))
        wts[U + GLU0:U + QK0] = pairs(columns(wval), columns(wgate))
        wts[U + QK0:U + V0] = np.concatenate([columns(wq), columns(wk)])
        wts[U + V0:U + G0] = wide(wv)
        wts[U + G0:U + MG0] = columns(wg)
        wts[U + MG0:U + RO0] = pairs(columns(wga), columns(wgb))
        wts[U + RO0:U + CO0] = columns(a["w_ret_o"][l])
        wts[U + CO0:U + WO0] = columns(a["w_conv_o"][l])
        wts[U + WO0:U + MIXER_UNITS] = columns(a["w_out"][l])
        j = l // 2
        if l % 2 == 0:
            up1, up3, dn = columns(a["dense_w1"][j]), columns(a["dense_w3"][j]), a["dense_w2"][j].reshape(-1, P, UNIT)
        else:
            up1 = np.concatenate([columns(w) for w in a["moe_w1"][j]])
            up3 = np.concatenate([columns(w) for w in a["moe_w3"][j]])
            dn = a["moe_w2"][j].reshape(-1, P, UNIT)
        F = FFN_CHUNKS[l]
        f = np.arange(F)
        at = U + MIXER_UNITS
        wts[at + 3 * f - (f > 0)] = up1
        wts[at + 3 * f + 1 - (f > 0)] = up3
        wts[at + 3 * (f + 1) + 1 - 2 * (f == F - 1)] = dn

    con = np.zeros((P, C_END), np.float32)
    half = QKD // 2
    inv_freq = np.float32(10000.0) ** (-np.arange(half, dtype=np.float32) / np.float32(half))
    ang = (np.arange(T, dtype=np.float32)[None, :] * inv_freq[:, None]).astype(np.float32)
    con[:, C_COS:C_COS + 2 * T] = np.tile(np.cos(ang), 2)
    con[:, C_SIN:C_SIN + 2 * T] = np.tile(np.sin(ang), 2)
    log_g = np.log1p(-np.exp2(-5.0 - np.arange(HEADS)))
    n, m = np.arange(T)[None, :], np.arange(T)[:, None]
    seen = n // CHUNK >= m // CHUNK
    for h in range(HEADS):
        dec = np.where(seen, np.exp(log_g[h] * np.abs(n - m)), 0.0) * QKD ** -0.5
        at = C_DEC + h * SCW
        con[:, at:at + T] = dec[0:P]
        con[:, at + T:at + SCW] = dec[P:, P:]
    con[:, C_IDENT:C_IDENT + P] = np.eye(P)
    con[:, C_ONES:C_ONES + P] = 1.0
    con[:, C_CW:C_VEC] = a["conv_w"].reshape(DEPTH, TAPS, KC, P).transpose(3, 0, 2, 1).reshape(P, -1)
    bg = a["b_gate"]
    vecs = [a["mix_norm"], a["conv_b"], a["conv_ln_g"], a["conv_ln_b"], bg[:, :D], bg[:, D:], a["b_conv_o"], a["ffn_norm"]]
    for i, w in enumerate(vecs):
        for l in range(DEPTH):
            at = C_VEC + (l * len(VECS) + i) * KC
            con[:, at:at + KC] = w[l].reshape(KC, P).T
    con[:, C_FIN:C_FIN + KC] = a["final_norm"].reshape(KC, P).T
    con[:, C_ROUT:C_SM] = a["moe_router"][0].reshape(KC, P, NEXP).transpose(1, 0, 2).reshape(P, -1)
    con[:, C_SM] = 1.0 / D
    con[:, C_SM + 1] = 1.0 / VD
    con[:, C_SM + 2] = EPS
    con[:, C_SM + 3:C_END] = np.arange(NEXP)
    xt = np.ascontiguousarray(a["x"].reshape(T, KC, P).transpose(2, 1, 0))

    nc = bacc.Bacc("TRN2", target_bir_lowering=False, num_devices=1)
    feeds = {"xt": xt, "wts": wts, "consts": con}
    args = [nc.dram_tensor(n, v.shape, F32, kind="ExternalInput").ap() for n, v in feeds.items()]
    args.append(nc.dram_tensor("out", (P, KC, T), F32, kind="ExternalOutput").ap())
    build(nc, *args)
    r = run(nc, [feeds], core_ids=[0])
    return np.asarray(r.results[0]["out"]).transpose(2, 1, 0).reshape(1, T, D)
```

```python
from contextlib import ExitStack

import numpy as np

import concourse.bass as bass
from concourse import mybir

P = 128
D = 1024
T = 256
DEPTH = 2
KC = D // P
TT = T // P
HEADS = 4
QKD = D // HEADS
VW = 2 * D
VD = VW // HEADS
VC = VW // P
CHUNK = 64
TAPS = 31
PAD = TAPS - 1
DFF = 2816
NEXP = 8
EFF = 1408
EPS = 1e-6

UNIT = 8 * P
RING = 4
N_GLU, N_QK, N_V, N_G, N_MG, N_RO, N_CO, N_WO = 16, 16, 16, 16, 16, 16, 8, 8
GLU0 = 0
QK0 = GLU0 + N_GLU
V0 = QK0 + N_QK
G0 = V0 + N_V
MG0 = G0 + N_G
RO0 = MG0 + N_MG
CO0 = RO0 + N_RO
WO0 = CO0 + N_CO
MIXER_UNITS = WO0 + N_WO
DENSE_CHUNKS = DFF // P
LAYER0 = (0, MIXER_UNITS + 3 * DENSE_CHUNKS)
UNITS = LAYER0[1] + MIXER_UNITS

ITEMS_MOST = NEXP + (2 * T) // (P + 1)
GROUPS = (3, 3, 3, 2)
assert sum(GROUPS) * P == EFF
BLOCKS = (("w1", 0), ("w3", 0), ("w1", 1), ("w3", 1), ("w2", 0), ("w1", 2), ("w3", 2), ("w2", 1),
          ("w1", 3), ("w3", 3), ("w2", 2), ("w2", 3))
NB = len(BLOCKS)
BIG = max(GROUPS) * D
LAST = min(GROUPS) * D
BIG_OF = {b: i for i, b in enumerate(b for b in BLOCKS if b[1] < 3)}
LAST_OF = {b: i for i, b in enumerate(b for b in BLOCKS if b[1] == 3)}
CHOSE_AT = 12
BRAW, BSPLIT = 4, 3

F32 = mybir.dt.float32
F32R = mybir.dt.float32r
U32 = mybir.dt.uint32
ALU = mybir.AluOpType
ACT = mybir.ActivationFunctionType

SCW = T + P
C_COS = 0
C_SIN = C_COS + 2 * T
C_DEC = C_SIN + 2 * T
C_IDENT = C_DEC + HEADS * SCW
C_ONES = C_IDENT + P
C_CW = C_ONES + P
C_VEC = C_CW + DEPTH * KC * TAPS
VECS = ("mix", "convb", "lng", "lnb", "bga", "bgb", "bco", "ffn")
C_FIN = C_VEC + DEPTH * len(VECS) * KC
C_ROUT = C_FIN + KC
C_SM = C_ROUT + KC * NEXP
C_TRI = C_SM + 3 + NEXP
C_IOTA = C_TRI + P
C_END = C_IOTA + P


def build(nc, xt, wts, big, last_group, consts, out):
    with ExitStack() as ctx:
        def sem(name):
            return ctx.enter_context(nc.semaphore(name))

        base = [nc.sbuf_base + (-nc.sbuf_base) % 64]
        places = {}

        def sb(name, shape, dt=F32, over=None, skip=0):
            size = 4 * int(np.prod(shape[1:]))
            if over is None:
                at = base[0]
                base[0] += size + (-size) % 64
                places[name] = (at, size)
            else:
                at, room = places[over]
                at += skip
                assert skip + size <= room, name
            return nc.alloc_sbuf_tensor_at(name, shape, dt, offset=at)

        x = sb("x", [P, KC, T])
        hnh = sb("hnh", [P, KC, T], F32R)
        hnl = sb("hnl", [P, KC, T], F32R)
        raw = sb("raw", [P, RING, UNIT])
        whi = sb("whi", [P, RING, UNIT], F32R)
        wlo = sb("wlo", [P, RING, UNIT], F32R)
        prob = sb("prob", [P, HEADS, SCW])
        rsq = sb("rsq", [P, 2, 4, T])
        q = sb("q", [P, HEADS, 2 * T])
        k = sb("k", [P, HEADS, 2 * T])
        v = sb("v", [P, HEADS, TT, VD])
        rh = sb("rh", [P, VC, T], F32R)
        g = sb("g", [P, VC, T])
        mga = sb("mga", [P, KC, T])
        mgb = sb("mgb", [P, KC, T])
        up = sb("up", [P, KC, PAD + T])
        cv = sb("cv", [P, KC, T])
        con = sb("con", [P, C_END])
        mtmp = sb("mtmp", [P, 2, T])
        diag = sb("diag", [P, HEADS, TT, P])
        small = sb("small", [P, 256])
        uh = sb("uh", [P, KC, T], F32R, over="q")
        ul = sb("ul", [P, KC, T], F32R, over="k")
        rl = sb("rl", [P, VC, T], F32R, over="v")
        mh = sb("mh", [P, KC, T], F32R, over="g")
        ml = sb("ml", [P, KC, T], F32R, over="g", skip=4 * KC * T)
        gated = sb("gated", [P, KC, T], F32, over="rsq")
        sig = sb("sig", [P, 2, T], F32, over="rh")
        rot = sb("rot", [P, 2, 2, 2 * T], F32, over="rh", skip=8 * T)
        xsq = sb("xsq", [P, KC, T], F32, over="mga")
        hn32 = sb("hn32", [P, KC, T], F32, over="mgb")
        lnsq = sb("lnsq", [P, KC, T], F32, over="up")
        yout = sb("yout", [P, KC, T], F32, over="cv")
        fs = sb("fs", [P, 2, T], F32, over="mga")
        f32_ = sb("f32_", [P, 2, T], F32, over="mga", skip=8 * T)
        fhh = sb("fhh", [P, 4, T], F32R, over="g")
        fhl = sb("fhl", [P, 4, T], F32R, over="g", skip=16 * T)
        def across(first, size):
            places[first + "+"] = (places[first][0], size)
            return first + "+"
        split_room = across("hnh", 2 * 4 * BSPLIT * BIG)
        assert places["hnh"][0] + places[split_room][1] <= places["q"][0]
        bhi = sb("bhi", [P, BSPLIT, BIG], F32R, over=split_room)
        blo = sb("blo", [P, BSPLIT, BIG], F32R, over=split_room, skip=4 * BSPLIT * BIG)
        assert places["q"][0] + 4 * BRAW * BIG <= places["g"][0]
        braw = sb("braw", [P, BRAW, BIG], F32, over=across("q", 4 * BRAW * BIG))
        hth = sb("hth", [P, TT, D], F32R, over="g")
        htl = sb("htl", [P, TT, D], F32R, over="g", skip=4 * TT * D)
        xgh = sb("xgh", [P, KC, P], F32R, over="mga")
        xgl = sb("xgl", [P, KC, P], F32R, over="mga", skip=4 * KC * P)
        ysh = sb("ysh", [P, D], F32R, over="cv")
        ysl = sb("ysl", [P, D], F32R, over="cv", skip=4 * D)
        act3 = sb("act3", [P, 3 * P], F32, over="up")
        inner = sb("inner", [P, 3 * P], F32, over="up", skip=12 * P)
        sel = sb("sel", [P, TT, P], F32R, over="up", skip=24 * P)
        selt = sb("selt", [P, T], F32R, over="up", skip=32 * P)
        ith = sb("ith", [P, 2, 3, P], F32R, over="up", skip=40 * P)
        itl = sb("itl", [P, 2, 3, P], F32R, over="diag")
        assert base[0] <= nc.sbuf_usable_end, base[0]

        pa = [ctx.enter_context(nc.psum_tensor(f"pa{i}", [P, 512], F32)) for i in range(4)]
        pb = [ctx.enter_context(nc.psum_tensor(f"pb{i}", [P, 512], F32)) for i in range(4)]

        cos2, sin2 = con[:, C_COS:C_COS + 2 * T], con[:, C_SIN:C_SIN + 2 * T]
        ident, ones = con[:, C_IDENT:C_IDENT + P], con[:, C_ONES:C_ONES + P]
        inv_d, inv_v, eps = (con[:, C_SM + i:C_SM + i + 1] for i in range(3))
        expert_no = con[:, C_SM + 3:C_SM + 3 + NEXP]
        before = con[:, C_TRI:C_TRI + P]
        slot_no = con[:, C_IOTA:C_IOTA + P]
        slot_of = small[:, 128:128 + 2 * 12].rearrange("p (i t) -> p i t", t=TT)
        gate_of = small[:, 152:152 + 2 * 12].rearrange("p (i t) -> p i t", t=TT)
        slot_gate = small[:, 176:177]
        plan = small[:, 180:184].bitcast(mybir.dt.int32)

        def vec(l, what, c):
            at = C_VEC + (l * len(VECS) + VECS.index(what)) * KC + c
            return con[:, at:at + 1]

        def tap(l, c, t):
            at = C_CW + (l * KC + c) * TAPS + t
            return con[:, at:at + 1]

        landed = [sem(f"landed{i}") for i in range(RING)]
        con_in, x_in, out_done = sem("con_in"), sem("x_in"), sem("out_done")
        hi_done, lo_done, unit_done = sem("hi_done"), sem("lo_done"), sem("unit_done")
        pad_zero = sem("pad_zero")
        sq_done, stat_done, rms_done, inv_done = sem("sq_done"), sem("stat_done"), sem("rms_done"), sem("inv_done")
        dg_done, bc_done = sem("dg_done"), sem("bc_done")
        n32_done, nh_done, nl_done = sem("n32_done"), sem("nh_done"), sem("nl_done")
        x_done = sem("x_done")
        sig_done, u_done = sem("sig_done"), sem("u_done")
        rot_step, qk_done = sem("rot_step"), sem("qk_done")
        va_done, vb_done = sem("va_done"), sem("vb_done")
        score_done, prob_done = sem("score_done"), sem("prob_done")
        g_done, pv_done, rsq_done, rg_done = sem("g_done"), sem("pv_done"), sem("rsq_done"), sem("rg_done")
        rstat_done, rrms_done, rinv_done, rdg_done, rbc_done = (sem(n) for n in (
            "rstat_done", "rrms_done", "rinv_done", "rdg_done", "rbc_done"))
        rn_done, rh_done, rl_done = sem("rn_done"), sem("rh_done"), sem("rl_done")
        mg_done = sem("mg_done")
        conv = sem("conv")
        lmean, lmeans, lmdg, lmbc, lcen = (sem(n) for n in ("lmean", "lmeans", "lmdg", "lmbc", "lcen"))
        lsq, lstat, lrms, linv, ldg, lbc, lnrm = (sem(n) for n in (
            "lsq", "lstat", "lrms", "linv", "ldg", "lbc", "lnrm"))
        lact, uh_done, ul_done = sem("lact"), sem("uh_done"), sem("ul_done")
        gated_done, mstep, mh_done, ml_done = sem("gated_done"), sem("mstep"), sem("mh_done"), sem("ml_done")
        fs_done, f32_done, fh_done, fl_done = sem("fs_done"), sem("f32_done"), sem("fh_done"), sem("fl_done")
        blanded = [sem(f"blanded{i}") for i in range(BRAW)]
        logit_done, top, ex_done = sem("logit_done"), sem("top"), sem("ex_done")
        tok_tr, tokh_done, tokl_done = sem("tok_tr"), sem("tokh_done"), sem("tokl_done")
        pos_done, plan_done, chosen = sem("pos_done"), sem("plan_done"), sem("chosen")
        gath_done, xgh_done, xgl_done = sem("gath_done"), sem("xgh_done"), sem("xgl_done")
        y_zero, st_done, str_done, trh_done = sem("y_zero"), sem("st_done"), sem("str_done"), sem("trh_done")
        yh_done, yl_done, scat_done, x_acc = sem("yh_done"), sem("yl_done"), sem("scat_done"), sem("x_acc")
        fin_done = sem("fin_done")

        block = ctx.enter_context(nc.Block())

        FF = DENSE_CHUNKS
        H1, H3, Y = pa[0], pa[1], pa[2:4]
        UP_AT = [BLOCKS.index(("w1", i)) for i in range(4)]

        def block_source(e, j):
            b = BLOCKS[j]
            if b[1] < 3:
                return big[e, BIG_OF[b]], BIG
            return last_group[e, LAST_OF[b]], LAST

        def cols(j):
            return GROUPS[BLOCKS[j][1]] * D

        def n_items(eng):
            eng.wait_ge(plan_done, 1)
            return eng.value_load(plan[0:1, 0:1], min_val=NEXP, max_val=ITEMS_MOST)

        @block.sync
        def _(sp):
            sp.dma_start(con[:, :], consts).then_inc(con_in, 16)

            def load(u, slot):
                sp.dma_start(raw[:, slot, :], wts[u]).then_inc(landed[slot], 16)
            for s in range(RING):
                load(s, s)
            n = UNITS // RING - 1
            with sp.Fori(0, n, 1) as it:
                for s in range(RING):
                    sp.wait_ge(lo_done, it * RING + (s + 1))
                    load(bass.ds(it * RING + (RING + s), 1), s)
            for s in range(UNITS % RING):
                sp.wait_ge(lo_done, n * RING + s + 1)
                load((n + 1) * RING + s, s)
            sp.wait_ge(unit_done, LAYER0[1] + WO0)

            def load_item(i, e):
                for j in range(NB):
                    sp.wait_ge(lo_done, i * NB + (UNITS + j - BRAW + 1))
                    src, w = block_source(e, j)
                    sp.dma_start(braw[:, j % BRAW, 0:w], src).then_inc(blanded[j % BRAW], 16)
            with sp.Fori(0, NEXP, 1) as e:
                load_item(e, bass.ds(e, 1))
            n = n_items(sp)
            with sp.If(n > NEXP):
                with sp.Fori(NEXP, n, 1) as i:
                    e = sp.value_load(plan[0:1, bass.ds(i - (NEXP - 1), 1)], min_val=0, max_val=NEXP - 1)
                    load_item(i, bass.ds(e, 1))
            for j in range(BSPLIT):
                sp.wait_ge(lo_done, n * NB + (UNITS + j - BRAW + 1))
                sp.sem_inc(blanded[j % BRAW], 16)
            sp.wait_ge(fin_done, 4)
            sp.dma_start(out, yout[:, :, :]).then_inc(out_done, 16)
            sp.wait_ge(out_done, 16)

        @block.gpsimd
        def _(pool):
            nc.gpsimd.memset(up[:, :, 0:PAD], 0.0).then_inc(pad_zero, 1)
            pool.wait_ge(lact, KC)
            nc.gpsimd.memset(up[:, :, 0:PAD], 0.0).then_inc(pad_zero, 1)

        @block.scalar
        def _(act):
            act.dma_start(x[:, :, :], xt).then_inc(x_in, 16)

            def split_hi(u):
                if isinstance(u, int) and u >= UNITS:
                    return
                act.wait_ge(landed[u % RING], 16 * (u // RING + 1))
                if u >= RING:
                    act.wait_ge(unit_done, u - RING + 1)
                nc.scalar.copy(whi[:, u % RING, :], raw[:, u % RING, :]).then_inc(hi_done, 1)

            def norm(n):
                for c in range(4):
                    if n == 0:
                        act.wait_ge(x_in, 16)
                    else:
                        act.wait_ge(x_done, 4 * (n - 1) + c + 1)
                    nc.scalar.activation(xsq[:, 2 * c:2 * c + 2, :], x[:, 2 * c:2 * c + 2, :],
                                         ACT.Square).then_inc(sq_done, 1)
                act.wait_ge(stat_done, n + 1)
                if n == 0:
                    act.wait_ge(con_in, 16)
                nc.scalar.activation(small[:, 0:TT], pb[2][:, 0:TT], ACT.Sqrt, bias=eps).then_inc(rms_done, 1)
                if n >= 2 * DEPTH - 1:
                    return
                for c in range(4):
                    act.wait_ge(n32_done, 8 * n + 2 * c + 2)
                    nc.scalar.copy(hnh[:, 2 * c:2 * c + 2, :], hn32[:, 2 * c:2 * c + 2, :]).then_inc(nh_done, 1)

            def mixer(l):
                U = LAYER0[l]
                for p in range(8):
                    split_hi(U + GLU0 + 2 * p + 4)
                    act.wait_ge(unit_done, U + GLU0 + 2 * p + 2)
                    if 8 * l + p >= 2:
                        act.wait_ge(u_done, 8 * l + p - 1)
                    nc.scalar.activation(sig[:, p % 2, :], pa[p % 4][:, T:2 * T], ACT.Sigmoid).then_inc(sig_done, 1)
                    split_hi(U + GLU0 + 2 * p + 5)
                for j in range(N_QK):
                    split_hi(U + QK0 + j + 4)
                for cg in range(4):
                    for j in range(3):
                        split_hi(U + V0 + 4 * cg + j + 4)
                    act.wait_ge(unit_done, U + V0 + 4 * cg + 4)
                    nc.scalar.copy(v[:, cg, 0, :], pa[(2 * cg) % 4][:, :]).then_inc(va_done, 1)
                    split_hi(U + V0 + 4 * cg + 7)
                def squares(h):
                    act.wait_ge(pv_done, 4 * l + h + 1)
                    if 4 * l + h >= 2:
                        act.wait_ge(rstat_done, 4 * l + h - 1)
                    for b in range(2):
                        nc.scalar.activation(rsq[:, h % 2, 2 * b:2 * b + 2, :], pb[b][:, :],
                                             ACT.Square).then_inc(rsq_done, 1)
                for p in range(8):
                    split_hi(U + G0 + 2 * p + 4)
                    act.wait_ge(unit_done, U + G0 + 2 * p + 2)
                    nc.scalar.activation(g[:, 2 * p:2 * p + 2, :], pa[p % 4][:, :], ACT.Silu).then_inc(g_done, 1)
                    split_hi(U + G0 + 2 * p + 5)
                    if p in (3, 5, 7):
                        squares((p - 3) // 2)
                for p in range(8):
                    split_hi(U + MG0 + 2 * p + 4)
                    act.wait_ge(unit_done, U + MG0 + 2 * p + 2)
                    nc.scalar.activation(mga[:, p, :], pa[p % 4][:, 0:T], ACT.Sigmoid, bias=vec(l, "bga", p))
                    nc.scalar.activation(mgb[:, p, :], pa[p % 4][:, T:2 * T], ACT.Sigmoid,
                                         bias=vec(l, "bgb", p)).then_inc(mg_done, 1)
                    split_hi(U + MG0 + 2 * p + 5)
                    if p == 0:
                        squares(3)
                    if p == 2:
                        act.wait_ge(rstat_done, 4 * l + 4)
                        nc.scalar.activation(small[:, 8:16], pb[2][:, 8:16], ACT.Sqrt, bias=eps).then_inc(rrms_done, 1)
                    if p >= 4:
                        h = p - 4
                        act.wait_ge(rn_done, 4 * l + h + 1)
                        nc.scalar.copy(rh[:, 4 * h:4 * h + 4, :], g[:, 4 * h:4 * h + 4, :]).then_inc(rh_done, 1)
                for j in range(N_RO):
                    split_hi(U + RO0 + j + 4)
                    if j == 2:
                        act.wait_ge(lmean, l + 1)
                        nc.scalar.copy(small[:, 32:34], pb[2][:, 32:34]).then_inc(lmeans, 1)
                    if 6 <= j < 10:
                        c = j - 6
                        act.wait_ge(lcen, 8 * l + 2 * c + 2)
                        nc.scalar.activation(lnsq[:, 2 * c:2 * c + 2, :], cv[:, 2 * c:2 * c + 2, :],
                                             ACT.Square).then_inc(lsq, 1)
                    if j == 11:
                        act.wait_ge(lstat, l + 1)
                        nc.scalar.activation(small[:, 36:38], pb[2][:, 36:38], ACT.Sqrt, bias=eps).then_inc(lrms, 1)
                    if j >= 14:
                        for c in range(4 * (j - 14), 4 * (j - 14) + 4):
                            act.wait_ge(lnrm, 8 * l + c + 1)
                            nc.scalar.activation(cv[:, c, :], cv[:, c, :], ACT.Silu, bias=vec(l, "lnb", c),
                                                 scale=vec(l, "lng", c)).then_inc(lact, 1)
                        for c in range(2 * (j - 14), 2 * (j - 14) + 2):
                            act.wait_ge(lact, 8 * l + 2 * c + 2)
                            nc.scalar.copy(uh[:, 2 * c:2 * c + 2, :], cv[:, 2 * c:2 * c + 2, :]).then_inc(uh_done, 1)
                for j in range(N_CO):
                    split_hi(U + CO0 + j + 4)
                    if j >= 1:
                        c = j - 1
                        act.wait_ge(mstep, 3 * (8 * l + c) + 3)
                        nc.scalar.copy(mh[:, c, :], cv[:, c, :]).then_inc(mh_done, 1)
                act.wait_ge(mstep, 3 * (8 * l + 7) + 3)
                nc.scalar.copy(mh[:, 7, :], cv[:, 7, :]).then_inc(mh_done, 1)
                for j in range(N_WO):
                    split_hi(U + WO0 + j + 4)

            def ffn():
                U, F = MIXER_UNITS, DENSE_CHUNKS
                for f in range(F):
                    if f:
                        split_hi(U + 3 * f + 3)
                    act.wait_ge(unit_done, U + 3 * f + 1 + (f == 0))
                    if f >= 2:
                        act.wait_ge(f32_done, f - 1)
                    nc.scalar.activation(fs[:, f % 2, :], pa[f % 4][:, 0:T], ACT.Silu).then_inc(fs_done, 1)
                    split_hi(U + 3 * f + 4)
                    act.wait_ge(f32_done, f + 1)
                    if f >= 4:
                        act.wait_ge(unit_done, U + 3 * (f - 4) + 5)
                    nc.scalar.copy(fhh[:, f % 4, :], f32_[:, f % 2, :]).then_inc(fh_done, 1)
                    split_hi(U + 3 * f + 5)
                split_hi(U + 3 * F + 3)

            def split_block(i, j):
                act.wait_ge(blanded[j % BRAW], i * (16 * NB // BRAW) + 16 * (j // BRAW + 1))
                act.wait_ge(unit_done, i * NB + (UNITS + j - BSPLIT + 1))
                w = cols(j % NB)
                nc.scalar.copy(bhi[:, j % BSPLIT, 0:w], braw[:, j % BRAW, 0:w]).then_inc(hi_done, 1)

            def tokens():
                for b in range(4):
                    act.wait_ge(tok_tr, b + 1)
                    nc.scalar.copy(hth[:, b // 2, (b % 2) * 512:(b % 2) * 512 + 512], pa[b][:, :]).then_inc(tokh_done, 1)

            def rows(i):
                act.wait_ge(gath_done, i + 1)
                nc.scalar.copy(slot_gate, pb[2][:, 0:1])
                for b in range(2):
                    nc.scalar.copy(xgh[:, 4 * b:4 * b + 4, :], pb[b][:, :]).then_inc(xgh_done, 1)

            def outputs(i):
                act.wait_ge(unit_done, i * NB + UNITS)
                for b in range(2):
                    nc.scalar.copy(ysh[:, b * 512:(b + 1) * 512], Y[b][:, :]).then_inc(yh_done, 1)

            def moe():
                for j in range(BSPLIT):
                    split_block(0, j)
                tokens()
                act.wait_ge(top, 4)
                nc.scalar.activation(small[:, 80:80 + TT], small[:, 76:76 + TT], ACT.Exp).then_inc(ex_done, 1)
                rows(0)
                nc.scalar.activation(small[:, 0:1], small[:, 1:2], ACT.Silu)
                n = n_items(act)
                act.wait_ge(y_zero, 2)
                with act.Fori(0, n, 1) as i:
                    outputs(i)
                    for j in range(NB):
                        if BLOCKS[j][0] == "w1":
                            gr = BLOCKS[j][1]
                            w = GROUPS[gr] * P
                            act.wait_ge(unit_done, i * NB + (UNITS + j + 1))
                            act.wait_ge(f32_done, i * 4 + (FF + gr))
                            nc.scalar.activation(act3[:, 0:w], H1[:, 0:w], ACT.Silu).then_inc(fs_done, 1)
                        if j in (2, 5, 8, 10):
                            gr = (2, 5, 8, 10).index(j)
                            w = GROUPS[gr]
                            act.wait_ge(trh_done, i * 4 + (gr + 1))
                            nc.scalar.copy(ith[:, gr % 2, 0:w, :], pb[3][:, 0:w * P]).then_inc(fh_done, 1)
                        if j == 10:
                            rows(i + 1)
                        split_block(i, j + BSPLIT)
                        if j == 1:
                            act.wait_ge(str_done, i + 1)
                            nc.scalar.copy(selt[:, :], pb[3][:, 0:T]).then_inc(st_done, 1)
                outputs(n)

            for s in range(4):
                split_hi(s)
            norm(0)
            mixer(0)
            norm(1)
            ffn()
            norm(2)
            mixer(1)
            norm(3)
            moe()
            norm(4)

        @block.vector
        def _(dve):
            def split_lo(u):
                if u >= UNITS:
                    return
                dve.wait_ge(hi_done, u + 1)
                if u >= RING:
                    dve.wait_ge(unit_done, u - RING + 1)
                nc.vector.tensor_tensor(wlo[:, u % RING, :], raw[:, u % RING, :],
                                        whi[:, u % RING, :].bitcast(F32), ALU.subtract).then_inc(lo_done, 1)

            def conv_ops(l, first, last):
                for n in range(first, min(last, KC * TAPS)):
                    c, t = 2 * (n // (2 * TAPS)) + n % 2, (n % (2 * TAPS)) // 2
                    if t == 0:
                        if n % 2 == 0:
                            dve.wait_ge(u_done, 8 * l + c + 2)
                        nc.vector.tensor_scalar(cv[:, c, :], up[:, c, 0:T], tap(l, c, 0), vec(l, "convb", c),
                                                ALU.mult, ALU.add).then_inc(conv, 1)
                        continue
                    dve.wait_ge(conv, l * KC * TAPS + n - 1)
                    nc.vector.scalar_tensor_tensor(out=cv[:, c, :], in0=up[:, c, t:t + T], scalar=tap(l, c, t),
                                                   in1=cv[:, c, :], op0=ALU.mult, op1=ALU.add).then_inc(conv, 1)

            def norm(n):
                dve.wait_ge(rms_done, n + 1)
                nc.vector.reciprocal(small[:, 4:4 + TT], small[:, 0:TT]).then_inc(inv_done, 1)
                dve.wait_ge(inv_done, n + 1)
                for t in range(TT):
                    nc.vector.tensor_scalar(diag[:, 0, t, :], ident, small[:, 4 + t:5 + t], None,
                                            ALU.mult).then_inc(dg_done, 1)
                dve.wait_ge(bc_done, n + 1)
                last = n == 2 * DEPTH
                for c in range(KC):
                    gain = con[:, C_FIN + c:C_FIN + c + 1] if last else vec(n // 2, ("mix", "ffn")[n % 2], c)
                    nc.vector.scalar_tensor_tensor(out=(yout if last else hn32)[:, c, :], in0=x[:, c, :], scalar=gain,
                                                   in1=pb[3][:, 0:T], op0=ALU.mult, op1=ALU.mult).then_inc(
                                                       fin_done if last and c % 2 else n32_done, 1)
                if n >= 2 * DEPTH - 1:
                    return
                for c in range(4):
                    dve.wait_ge(nh_done, 4 * n + c + 1)
                    nc.vector.tensor_tensor(hnl[:, 2 * c:2 * c + 2, :], hn32[:, 2 * c:2 * c + 2, :],
                                            hnh[:, 2 * c:2 * c + 2, :].bitcast(F32), ALU.subtract).then_inc(nl_done, 1)

            def mixer(l):
                U = LAYER0[l]
                for p in range(8):
                    split_lo(U + GLU0 + 2 * p + 4)
                    dve.wait_ge(sig_done, 8 * l + p + 1)
                    if p == 0:
                        dve.wait_ge(pad_zero, l + 1)
                    nc.vector.tensor_tensor(up[:, p, PAD:], pa[p % 4][:, 0:T], sig[:, p % 2, :],
                                            ALU.mult).then_inc(u_done, 1)
                    split_lo(U + GLU0 + 2 * p + 5)
                    conv_ops(l, 6 * max(0, p - 3), 6 * max(0, p - 2))
                done = 30
                for p in range(8):
                    dst, h = (q, p) if p < 4 else (k, p - 4)
                    split_lo(U + QK0 + 2 * p + 4)
                    dve.wait_ge(unit_done, U + QK0 + 2 * p + 2)
                    if p >= 2 or l:
                        dve.wait_ge(qk_done, 2 * (8 * l + p - 1))
                    nc.vector.tensor_tensor(rot[:, p % 2, 0, :], pa[p % 4][:, :], cos2, ALU.mult).then_inc(rot_step, 1)
                    nc.vector.tensor_tensor(rot[:, p % 2, 1, :], pa[p % 4][:, :], sin2, ALU.mult).then_inc(rot_step, 1)
                    conv_ops(l, done, done + 2)
                    split_lo(U + QK0 + 2 * p + 5)
                    dve.wait_ge(rot_step, 2 * (8 * l + p + 1))
                    nc.vector.tensor_tensor(dst[:, h, 0:T], rot[:, p % 2, 0, 0:T], rot[:, p % 2, 1, T:],
                                            ALU.subtract).then_inc(qk_done, 1)
                    nc.vector.tensor_tensor(dst[:, h, T:], rot[:, p % 2, 1, 0:T], rot[:, p % 2, 0, T:],
                                            ALU.add).then_inc(qk_done, 1)
                    done += 2
                for cg in range(4):
                    for j in range(3):
                        split_lo(U + V0 + 4 * cg + j + 4)
                        conv_ops(l, done, done + 4)
                        done += 4
                    dve.wait_ge(unit_done, U + V0 + 4 * cg + 4)
                    nc.vector.tensor_copy(v[:, cg, 1, :], pa[(2 * cg + 1) % 4][:, :]).then_inc(vb_done, 1)
                    split_lo(U + V0 + 4 * cg + 7)
                    conv_ops(l, done, done + 3)
                    done += 3
                for h in range(HEADS):
                    dve.wait_ge(score_done, 4 * l + h + 1)
                    nc.vector.tensor_tensor(prob[:, h, :], pb[h][:, 0:SCW], con[:, C_DEC + h * SCW:C_DEC + (h + 1) * SCW],
                                            ALU.mult).then_inc(prob_done, 1)
                conv_ops(l, done, done + 6)
                done += 6

                def gate_r(h):
                    dve.wait_ge(pv_done, 4 * l + h + 1)
                    dve.wait_ge(g_done, 8 * l + 2 * h + 2)
                    for b in range(2):
                        c = 4 * h + 2 * b
                        dve.wait_ge(rsq_done, 8 * l + 2 * h + b + 1)
                        nc.vector.tensor_tensor(g[:, c:c + 2, :], pb[b][:, :].rearrange("p (c t) -> p c t", c=2),
                                                g[:, c:c + 2, :], ALU.mult).then_inc(rg_done, 1)
                for p in range(8):
                    split_lo(U + G0 + 2 * p + 4)
                    conv_ops(l, done, done + 5)
                    done += 5
                    split_lo(U + G0 + 2 * p + 5)
                    conv_ops(l, done, done + 4)
                    done += 4
                    if p in (3, 5, 7):
                        gate_r((p - 3) // 2)
                for p in range(8):
                    split_lo(U + MG0 + 2 * p + 4)
                    if p == 0:
                        gate_r(3)
                    if p == 2:
                        dve.wait_ge(rrms_done, l + 1)
                        nc.vector.reciprocal(small[:, 16:24], small[:, 8:16]).then_inc(rinv_done, 1)
                        dve.wait_ge(rinv_done, l + 1)
                        for h in range(HEADS):
                            for t in range(TT):
                                nc.vector.tensor_scalar(diag[:, h, t, :], ident, small[:, 16 + 2 * h + t:17 + 2 * h + t],
                                                        None, ALU.mult).then_inc(rdg_done, 1)
                    if p >= 4:
                        h = p - 4
                        dve.wait_ge(rbc_done, 4 * l + 4)
                        bc = pb[h // 2][:, (h % 2) * T:(h % 2) * T + T]
                        nc.vector.tensor_tensor(g[:, 4 * h:4 * h + 4, :], g[:, 4 * h:4 * h + 4, :],
                                                bc.rearrange("p (o t) -> p o t", o=1).broadcast_to([P, 4, T]),
                                                ALU.mult).then_inc(rn_done, 1)
                    conv_ops(l, done, done + 4)
                    done += 4
                    split_lo(U + MG0 + 2 * p + 5)
                    conv_ops(l, done, done + 3)
                    done += 3
                    if p >= 4:
                        dve.wait_ge(rh_done, 4 * l + h + 1)
                        nc.vector.tensor_tensor(rl[:, 4 * h:4 * h + 4, :], g[:, 4 * h:4 * h + 4, :],
                                                rh[:, 4 * h:4 * h + 4, :].bitcast(F32), ALU.subtract).then_inc(rl_done, 1)
                conv_ops(l, done, KC * TAPS)
                for j in range(N_RO):
                    split_lo(U + RO0 + j + 4)
                    if j % 2 == 1:
                        c = j // 2
                        dve.wait_ge(unit_done, U + RO0 + j + 1)
                        if c == 0:
                            dve.wait_ge(mg_done, 8 * l + 8)
                        nc.vector.tensor_tensor(gated[:, c, :], pa[c % 4][:, 0:T],
                                                mga[:, c, :], ALU.mult).then_inc(gated_done, 1)
                    if j == 3:
                        dve.wait_ge(lmeans, l + 1)
                        for t in range(TT):
                            nc.vector.tensor_scalar(diag[:, 0, t, :], ident, small[:, 32 + t:33 + t], None,
                                                    ALU.mult).then_inc(lmdg, 1)
                    if j == 5:
                        dve.wait_ge(lmbc, l + 1)
                        for c in range(KC):
                            nc.vector.tensor_tensor(cv[:, c, :], cv[:, c, :], pb[3][:, 0:T], ALU.subtract).then_inc(lcen, 1)
                    if j == 11:
                        dve.wait_ge(lrms, l + 1)
                        nc.vector.reciprocal(small[:, 40:42], small[:, 36:38]).then_inc(linv, 1)
                        dve.wait_ge(linv, l + 1)
                        for t in range(TT):
                            nc.vector.tensor_scalar(diag[:, 1, t, :], ident, small[:, 40 + t:41 + t], None,
                                                    ALU.mult).then_inc(ldg, 1)
                    if j == 13:
                        dve.wait_ge(lbc, l + 1)
                        for c in range(KC):
                            nc.vector.tensor_tensor(cv[:, c, :], cv[:, c, :], pb[3][:, T:2 * T], ALU.mult).then_inc(lnrm, 1)
                    if j >= 14:
                        for c in range(2 * (j - 14), 2 * (j - 14) + 2):
                            dve.wait_ge(uh_done, 4 * l + c + 1)
                            nc.vector.tensor_tensor(ul[:, 2 * c:2 * c + 2, :], cv[:, 2 * c:2 * c + 2, :],
                                                    uh[:, 2 * c:2 * c + 2, :].bitcast(F32), ALU.subtract).then_inc(ul_done, 1)

                def merged_lo(c):
                    dve.wait_ge(mh_done, 8 * l + c + 1)
                    nc.vector.tensor_tensor(ml[:, c, :], cv[:, c, :], mh[:, c, :].bitcast(F32),
                                            ALU.subtract).then_inc(ml_done, 1)
                for c in range(N_CO):
                    n = 3 * (8 * l + c)
                    dve.wait_ge(unit_done, U + CO0 + c + 1)
                    nc.vector.scalar_tensor_tensor(out=mtmp[:, c % 2, :], in0=pa[c % 4][:, 0:T],
                                                   scalar=vec(l, "bco", c), in1=mgb[:, c, :], op0=ALU.add,
                                                   op1=ALU.mult).then_inc(mstep, 1)
                    dve.wait_ge(ul_done, 4 * l + 4)
                    dve.wait_ge(mstep, n + 1)
                    nc.vector.tensor_tensor(cv[:, c, :], mtmp[:, c % 2, :], gated[:, c, :], ALU.add).then_inc(mstep, 2)
                    split_lo(U + CO0 + c + 4)
                    if c >= 1:
                        merged_lo(c - 1)
                merged_lo(7)
                for p in range(4):
                    split_lo(U + WO0 + 2 * p + 4)
                    dve.wait_ge(unit_done, U + WO0 + 2 * p + 2)
                    xx = x[:, 2 * p:2 * p + 2, :]
                    nc.vector.tensor_tensor(xx, pa[p % 4][:, :].rearrange("p (c t) -> p c t", c=2), xx,
                                            ALU.add).then_inc(x_done, 1)
                    split_lo(U + WO0 + 2 * p + 5)

            def ffn():
                U, F = MIXER_UNITS, DENSE_CHUNKS
                for f in range(F):
                    if f:
                        split_lo(U + 3 * f + 3)
                    dve.wait_ge(fs_done, f + 1)
                    nc.vector.tensor_tensor(f32_[:, f % 2, :], fs[:, f % 2, :], pa[f % 4][:, T:2 * T],
                                            ALU.mult).then_inc(f32_done, 1)
                    split_lo(U + 3 * f + 4)
                    dve.wait_ge(fh_done, f + 1)
                    nc.vector.tensor_tensor(fhl[:, f % 4, :], f32_[:, f % 2, :], fhh[:, f % 4, :].bitcast(F32),
                                            ALU.subtract).then_inc(fl_done, 1)
                    split_lo(U + 3 * f + 5)
                split_lo(U + 3 * F + 3)
                dve.wait_ge(unit_done, U + 3 * F)
                for p in range(4):
                    xx = x[:, 2 * p:2 * p + 2, :]
                    nc.vector.tensor_tensor(xx, pb[p][:, :].rearrange("p (c t) -> p c t", c=2), xx,
                                            ALU.add).then_inc(x_done, 1)

            def split_block(i, j):
                dve.wait_ge(hi_done, i * NB + (UNITS + j + 1))
                w = cols(j % NB)
                nc.vector.tensor_tensor(blo[:, j % BSPLIT, 0:w], braw[:, j % BRAW, 0:w],
                                        bhi[:, j % BSPLIT, 0:w].bitcast(F32), ALU.subtract).then_inc(lo_done, 1)

            def tokens():
                for b in range(4):
                    dve.wait_ge(tokh_done, b + 1)
                    at = slice((b % 2) * 512, (b % 2) * 512 + 512)
                    nc.vector.tensor_tensor(htl[:, b // 2, at], pa[b][:, :], hth[:, b // 2, at].bitcast(F32),
                                            ALU.subtract).then_inc(tokl_done, 1)

            def route():
                lg, mx, ix = small[:, 48:64], small[:, 84:100], small[:, 100:116].bitcast(U32)
                step = [0]

                def then(ins, wait=False):
                    ins.then_inc(top, 1)
                    step[0] += 1
                    if wait:
                        dve.wait_ge(top, step[0])
                dve.wait_ge(tokl_done, 4)
                nc.vector.memset(Y[0][:, :], 0.0).then_inc(y_zero, 1)
                nc.vector.memset(Y[1][:, :], 0.0).then_inc(y_zero, 1)
                nc.vector.memset(selt[:, :].bitcast(F32), 0.0).then_inc(st_done, 1)
                dve.wait_ge(logit_done, 1)
                then(nc.vector.tensor_copy(lg, pb[2][:, 48:64]), True)
                for t in range(TT):
                    then(nc.vector.max(mx[:, 8 * t:8 * t + 8], lg[:, 8 * t:8 * t + 8]), t == TT - 1)
                m = mx.rearrange("p (t e) -> p t e", t=TT)
                then(nc.vector.tensor_tensor(small[:, 76:78].rearrange("p (t o) -> p t o", o=1), m[:, :, 1:2],
                                             m[:, :, 0:1], ALU.subtract))
                for t in range(TT):
                    then(nc.vector.max_index(ix[:, 8 * t:8 * t + 8], mx[:, 8 * t:8 * t + 8],
                                             lg[:, 8 * t:8 * t + 8]), t == TT - 1)
                ixf = small[:, 116:120]
                then(nc.vector.tensor_copy(ixf.rearrange("p (k t) -> p t k", k=2),
                                           ix.rearrange("p (t e) -> p t e", t=TT)[:, :, 0:2]), True)
                one, two, chose = small[:, 184:200], small[:, 200:216], small[:, 216:232]
                for t in range(TT):
                    at = slice(8 * t, 8 * t + 8)
                    then(nc.vector.tensor_scalar(one[:, at], expert_no, ixf[:, t:t + 1], None, ALU.is_equal))
                    then(nc.vector.tensor_scalar(two[:, at], expert_no, ixf[:, 2 + t:3 + t], None, ALU.is_equal),
                         t == TT - 1)
                then(nc.vector.tensor_tensor(chose, one, two, ALU.add))
                chose_at = step[0]
                dve.wait_ge(ex_done, 1)
                e = small[:, 80:80 + TT]
                then(nc.vector.tensor_scalar(small[:, 82:84], e, 1.0, None, ALU.add), True)
                wt = small[:, 120:124]
                then(nc.vector.reciprocal(wt[:, 0:2], small[:, 82:84]), True)
                then(nc.vector.tensor_tensor(wt[:, 2:4], wt[:, 0:2], e, ALU.mult), True)
                for t in range(TT):
                    at = slice(8 * t, 8 * t + 8)
                    then(nc.vector.tensor_scalar(one[:, at], one[:, at], wt[:, t:t + 1], None, ALU.mult), t == TT - 1)
                for t in range(TT):
                    at = slice(8 * t, 8 * t + 8)
                    nc_out = gate_of[:, 0:NEXP, t]
                    then(nc.vector.scalar_tensor_tensor(out=nc_out, in0=two[:, at], scalar=wt[:, 2 + t:3 + t],
                                                        in1=one[:, at], op0=ALU.mult, op1=ALU.add))
                dve.wait_ge(pos_done, 1)
                over, rank, junk = small[:, 84:92], small[:, 92:100], small[:, 232:240]
                then(nc.vector.tensor_scalar(over, pb[2][:, 80:88], float(P), None, ALU.is_gt))
                for t in range(TT):
                    at = slice(8 * t, 8 * t + 8)
                    then(nc.vector.scalar_tensor_tensor(out=lg[:, at], in0=pb[2][:, 64 + 8 * t:72 + 8 * t], scalar=1.0,
                                                        in1=chose[:, at], op0=ALU.add, op1=ALU.mult), t == TT - 1)
                for t in range(TT):
                    then(nc.vector.tensor_scalar(slot_of[:, 0:NEXP, t], lg[:, 8 * t:8 * t + 8], -1.0, None, ALU.add),
                         t == TT - 1)
                pick(0)
                then(nc.vector.tensor_tensor_scan(rank, over, over, 0.0, ALU.add, ALU.max), True)
                pf = small[:, 240:244]
                then(nc.vector.tensor_scalar(pf[:, 0:1], rank[:, 7:8], float(NEXP), None, ALU.add))
                for m in range(ITEMS_MOST - NEXP):
                    one8 = small[:, 184 + 8 * m:192 + 8 * m]
                    then(nc.vector.scalar_tensor_tensor(out=one8, in0=rank, scalar=float(m + 1), in1=over,
                                                        op0=ALU.is_equal, op1=ALU.mult), True)
                    then(nc.vector.tensor_tensor_reduce(junk, one8, expert_no, 1.0, 0.0, ALU.mult, ALU.add,
                                                        pf[:, 1 + m:2 + m]), True)
                    for t in range(TT):
                        then(nc.vector.tensor_tensor_reduce(junk, one8, slot_of[:, 0:NEXP, t], 1.0, float(-P), ALU.mult,
                                                            ALU.add, slot_of[:, NEXP + m, t:t + 1]), True)
                        then(nc.vector.tensor_tensor_reduce(junk, one8, gate_of[:, 0:NEXP, t], 1.0, 0.0, ALU.mult,
                                                            ALU.add, gate_of[:, NEXP + m, t:t + 1]), True)
                nc.vector.memset(slot_of[:, ITEMS_MOST, :], -1.0)
                nc.vector.memset(gate_of[:, ITEMS_MOST, :], 0.0)
                nc.vector.tensor_copy(plan, pf).then_inc(plan_done, 1)
                return chose_at

            def pick(i):
                for t in range(TT):
                    where = slot_of[:, i, t:t + 1] if isinstance(i, int) else \
                        slot_of[:, bass.ds(i, 1), t:t + 1].rearrange("p i t -> p (i t)")
                    nc.vector.tensor_scalar(sel[:, t, :], slot_no, where, None, ALU.is_equal).then_inc(chosen, 1)

            def rows(i):
                for b in range(2):
                    dve.wait_ge(xgh_done, i * 2 + (b + 1))
                    nc.vector.tensor_tensor(xgl[:, 4 * b:4 * b + 4, :], pb[b][:, :].rearrange("p (c s) -> p c s", c=4),
                                            xgh[:, 4 * b:4 * b + 4, :].bitcast(F32), ALU.subtract).then_inc(xgl_done, 1)

            def outputs(i):
                for b in range(2):
                    dve.wait_ge(yh_done, i * 2 + (b + 1))
                    at = slice(b * 512, (b + 1) * 512)
                    nc.vector.tensor_tensor(ysl[:, at], Y[b][:, :], ysh[:, at].bitcast(F32),
                                            ALU.subtract).then_inc(yl_done, 1)

            def accumulate(i, done):
                for p in range(4):
                    dve.wait_ge(scat_done, i * 4 + (p + 1))
                    xx = x[:, 2 * p:2 * p + 2, :]
                    nc.vector.tensor_tensor(xx, pb[p % 3][:, :].rearrange("p (c t) -> p c t", c=2), xx,
                                            ALU.add).then_inc(done, 1)

            def moe():
                for j in range(BSPLIT):
                    split_block(0, j)
                tokens()
                route()
                rows(0)
                n = n_items(dve)
                with dve.Fori(0, n, 1) as i:
                    outputs(i)
                    for j in range(NB):
                        if BLOCKS[j][0] == "w3":
                            gr = BLOCKS[j][1]
                            w = GROUPS[gr] * P
                            dve.wait_ge(unit_done, i * NB + (UNITS + j + 1))
                            dve.wait_ge(fs_done, i * 4 + (FF + gr + 1))
                            nc.vector.scalar_tensor_tensor(out=inner[:, 0:w], in0=act3[:, 0:w], scalar=slot_gate,
                                                           in1=H3[:, 0:w], op0=ALU.mult, op1=ALU.mult).then_inc(f32_done, 1)
                        if j == 1:
                            accumulate(i, x_acc)
                        if j in (2, 5, 8, 10):
                            gr = (2, 5, 8, 10).index(j)
                            w = GROUPS[gr]
                            dve.wait_ge(fh_done, i * 4 + (FF + gr + 1))
                            nc.vector.tensor_tensor(itl[:, gr % 2, 0:w, :],
                                                    pb[3][:, 0:w * P].rearrange("p (c s) -> p c s", c=w),
                                                    ith[:, gr % 2, 0:w, :].bitcast(F32), ALU.subtract).then_inc(fl_done, 1)
                        if j == 9:
                            dve.wait_ge(str_done, i + 1)
                            pick(i + 1)
                        if j == 10:
                            rows(i + 1)
                        split_block(i, j + BSPLIT)
                outputs(n)
                accumulate(n, x_done)

            dve.wait_ge(con_in, 16)
            dve.wait_ge(x_in, 16)
            for s in range(4):
                split_lo(s)
            norm(0)
            mixer(0)
            norm(1)
            ffn()
            norm(2)
            mixer(1)
            norm(3)
            moe()
            norm(4)

        @block.tensor
        def _(pe):
            mm = nc.tensor.matmul

            def tiles(u, dst, xh, xl, kind="m", first=True, last=True):
                s = u % RING
                pe.wait_ge(hi_done, u + 1)
                for i in range(8):
                    w = whi[:, s, i * P:(i + 1) * P]
                    mm(dst(i), w, xh(i), start=first(i), stop=False, skip_group_check=True)
                    mm(dst(i), w, xl(i), start=False, stop=False, skip_group_check=True)
                pe.wait_ge(lo_done, u + 1)
                for i in range(8):
                    ins = mm(dst(i), wlo[:, s, i * P:(i + 1) * P], xh(i), start=False, stop=last(i),
                             skip_group_check=True)
                ins.then_inc(unit_done, 1)

            def project(u, dst, ah, al, k0=0, first=True, last=True):
                tiles(u, lambda i: dst, lambda i: ah[:, k0 + i, :], lambda i: al[:, k0 + i, :],
                      first=lambda i: first and i == 0, last=lambda i: last and i == 7)

            def stat(dst, src, cols, scale, done):
                for t in range(TT):
                    for i, c in enumerate(cols):
                        ins = mm(dst[:, t:t + 1], src(c)[:, t * P:(t + 1) * P], scale, start=i == 0,
                                 stop=i == len(cols) - 1)
                ins.then_inc(done, 1)

            def spread(dst, d, done):
                mm(dst, ones, d.rearrange("p t n -> p (t n)"), start=True, stop=True).then_inc(done, 1)

            def norm(n):
                if n == 0:
                    pe.wait_ge(con_in, 16)
                elif n % 2 == 0:
                    pe.wait_ge(x_done, 4 * n)
                for t in range(TT):
                    for c in range(KC):
                        if t == 0 and c % 2 == 0:
                            pe.wait_ge(sq_done, 4 * n + c // 2 + 1)
                        ins = mm(pb[2][:, t:t + 1], xsq[:, c, t * P:(t + 1) * P], inv_d, start=c == 0, stop=c == KC - 1)
                ins.then_inc(stat_done, 1)
                pe.wait_ge(dg_done, 2 * n + 2)
                spread(pb[3][:, 0:T], diag[:, 0, :, :], bc_done)
                if n < 2 * DEPTH - 1:
                    pe.wait_ge(nh_done, 4 * n + 4)
                    pe.wait_ge(nl_done, 4 * n + 4)

            def mixer(l):
                U = LAYER0[l]

                def half(j):
                    return pa[(j // 2) % 4][:, (j % 2) * T:(j % 2) * T + T]

                for j in range(N_GLU):
                    project(U + GLU0 + j, half(j), hnh, hnl)
                for j in range(N_QK):
                    project(U + QK0 + j, half(j), hnh, hnl)
                for cg in range(4):
                    for j in range(4):
                        u = U + V0 + 4 * cg + j
                        s = u % RING
                        pe.wait_ge(hi_done, u + 1)
                        for part in range(2):
                            if part:
                                pe.wait_ge(lo_done, u + 1)
                            for kk in range(2):
                                w = (wlo if part else whi)[:, s, kk * 512:(kk + 1) * 512]
                                for t in range(TT):
                                    dst = pa[(2 * cg + t) % 4][:, :]
                                    for a in ((hnh,) if part else (hnh, hnl)):
                                        ins = mm(dst, a[:, 2 * j + kk, t * P:(t + 1) * P], w,
                                                 start=j == 0 and kk == 0 and part == 0 and a is hnh,
                                                 stop=j == 3 and part == 1 and kk == 1, skip_group_check=True)
                        ins.then_inc(unit_done, 1)
                pe.wait_ge(qk_done, 16 * l + 16)
                for h in range(HEADS):
                    for t in range(TT):
                        n0, dst = t * P, pb[h][:, 0:T] if t == 0 else pb[h][:, T:SCW]
                        for c in range(2):
                            ins = mm(dst, k[:, h, c * T + t * P:c * T + (t + 1) * P], q[:, h, c * T + n0:(c + 1) * T],
                                     start=c == 0, stop=c == 1)
                    ins.then_inc(score_done, 1)

                def pv(h):
                    pe.wait_ge(prob_done, 4 * l + 4)
                    pe.wait_ge(va_done, 4 * l + h + 1)
                    pe.wait_ge(vb_done, 4 * l + h + 1)
                    if h:
                        pe.wait_ge(rg_done, 8 * l + 2 * h)
                        pe.wait_ge(rsq_done, 8 * l + 2 * h)
                    for e in range(4):
                        dst = pb[e // 2]
                        o = (e % 2) * T
                        mm(dst[:, o:o + T], v[:, h, 0, e * P:(e + 1) * P], prob[:, h, 0:T], start=True, stop=True)
                        ins = mm(dst[:, o + P:o + T], v[:, h, 1, e * P:(e + 1) * P], prob[:, h, T:SCW], start=False,
                                 stop=True, skip_group_check=True)
                    ins.then_inc(pv_done, 1)

                def rstat(h):
                    pe.wait_ge(rsq_done, 8 * l + 2 * h + 2)
                    stat(pb[2][:, 8 + 2 * h:10 + 2 * h], lambda c: rsq[:, h % 2, c, :], range(4), inv_v, rstat_done)
                for p in range(8):
                    project(U + G0 + 2 * p, half(2 * p), hnh, hnl)
                    project(U + G0 + 2 * p + 1, half(2 * p + 1), hnh, hnl)
                    if p in (2, 4, 6):
                        pv((p - 2) // 2)
                    if p in (5, 7):
                        rstat((p - 5) // 2)
                for p in range(8):
                    project(U + MG0 + 2 * p, half(2 * p), hnh, hnl)
                    project(U + MG0 + 2 * p + 1, half(2 * p + 1), hnh, hnl)
                    if p == 0:
                        rstat(2)
                        pv(3)
                    if p == 1:
                        rstat(3)
                    if p == 3:
                        for h in range(HEADS):
                            if h == 0:
                                pe.wait_ge(rg_done, 8 * l + 8)
                                pe.wait_ge(rsq_done, 8 * l + 8)
                            pe.wait_ge(rdg_done, 8 * l + 2 * h + 2)
                            spread(pb[h // 2][:, (h % 2) * T:(h % 2) * T + T], diag[:, h, :, :], rbc_done)
                pe.wait_ge(rh_done, 4 * l + 4)
                pe.wait_ge(rl_done, 4 * l + 4)
                for j in range(N_RO):
                    c = j // 2
                    project(U + RO0 + j, pa[c % 4][:, 0:T], rh, rl, k0=8 * (j % 2), first=j % 2 == 0, last=j % 2 == 1)
                    if j == 1:
                        pe.wait_ge(conv, (l + 1) * KC * TAPS)
                        stat(pb[2][:, 32:34], lambda c: cv[:, c, :], range(KC), inv_d, lmean)
                    if j == 4:
                        pe.wait_ge(lmdg, 2 * l + 2)
                        spread(pb[3][:, 0:T], diag[:, 0, :, :], lmbc)
                    if j == 10:
                        pe.wait_ge(lsq, 4 * l + 4)
                        stat(pb[2][:, 36:38], lambda c: lnsq[:, c, :], range(KC), inv_d, lstat)
                    if j == 12:
                        pe.wait_ge(ldg, 2 * l + 2)
                        spread(pb[3][:, T:2 * T], diag[:, 1, :, :], lbc)
                pe.wait_ge(uh_done, 4 * l + 4)
                pe.wait_ge(ul_done, 4 * l + 4)
                for j in range(N_CO):
                    if j >= 4:
                        pe.wait_ge(mstep, 3 * (8 * l + j - 4) + 1)
                    project(U + CO0 + j, pa[j % 4][:, 0:T], uh, ul)
                pe.wait_ge(mh_done, 8 * l + 8)
                pe.wait_ge(ml_done, 8 * l + 8)
                for j in range(N_WO):
                    project(U + WO0 + j, half(j), mh, ml)

            def ffn():
                U, F = MIXER_UNITS, DENSE_CHUNKS

                def down(f, u):
                    pe.wait_ge(fh_done, f + 1)
                    pe.wait_ge(fl_done, f + 1)
                    tiles(u, lambda i: pb[i // 2][:, (i % 2) * T:(i % 2) * T + T], lambda i: fhh[:, f % 4, :],
                          lambda i: fhl[:, f % 4, :], first=lambda i: f == 0 and i % 2 == 0,
                          last=lambda i: f == F - 1)
                for f in range(F + 1):
                    if f < F:
                        u = U + 3 * f - (f > 0)
                        project(u, pa[f % 4][:, 0:T], hnh, hnl)
                        project(u + 1, pa[f % 4][:, T:2 * T], hnh, hnl)
                    if f:
                        down(f - 1, U + 3 * f + 1 - (f == F) * 2)

            def route():
                pe.wait_ge(n32_done, 8 * 3 + 8)
                for t in range(TT):
                    for c in range(KC):
                        ins = mm(pb[2][:, 48 + 8 * t:56 + 8 * t], hn32[:, c, t * P:(t + 1) * P],
                                 con[:, C_ROUT + c * NEXP:C_ROUT + (c + 1) * NEXP], start=c == 0, stop=c == KC - 1)
                ins.then_inc(logit_done, 1)
                pe.wait_ge(x_done, 12)
                for b in range(4):
                    for i in range(4):
                        c = 4 * (b % 2) + i
                        ins = nc.tensor.transpose(pa[b][:, i * P:(i + 1) * P], hn32[:, c, (b // 2) * P:(b // 2 + 1) * P], ident)
                    ins.then_inc(tok_tr, 1)
                pe.wait_ge(top, CHOSE_AT)
                chose = small[:, 216:232]
                at = [pb[2][:, 64 + 8 * i:72 + 8 * i] for i in range(3)]
                mm(at[0], before, chose[:, 0:8], start=True, stop=True)
                mm(at[1], ones, chose[:, 0:8], start=True, stop=False)
                mm(at[1], before, chose[:, 8:16], start=False, stop=True)
                mm(at[2], ones, chose[:, 0:8], start=True, stop=False)
                mm(at[2], ones, chose[:, 8:16], start=False, stop=True).then_inc(pos_done, 1)

            def gather(i):
                for c in range(KC):
                    dst = pb[c // 4][:, (c % 4) * P:(c % 4 + 1) * P]
                    for t in range(TT):
                        mm(dst, hth[:, t, c * P:(c + 1) * P], sel[:, t, :], start=t == 0, stop=False)
                        mm(dst, htl[:, t, c * P:(c + 1) * P], sel[:, t, :], start=False, stop=t == TT - 1)
                for t in range(TT):
                    gate = gate_of[:, i, t:t + 1] if isinstance(i, int) else \
                        gate_of[:, bass.ds(i, 1), t:t + 1].rearrange("p i t -> p (i t)")
                    ins = mm(pb[2][:, 0:1], sel[:, t, :].bitcast(F32), gate, start=t == 0, stop=t == TT - 1)
                ins.then_inc(gath_done, 1)

            def scatter(i):
                pe.wait_ge(yh_done, i * 2 + 2)
                pe.wait_ge(yl_done, i * 2 + 2)
                pe.wait_ge(st_done, i + 1)
                for p in range(4):
                    if p == 3:
                        pe.wait_ge(x_acc if not p_last[0] else x_done, (i * 4 + 1) if not p_last[0] else 13)
                    for c in (2 * p, 2 * p + 1):
                        dst = pb[p % 3][:, (c % 2) * T:(c % 2) * T + T]
                        mm(dst, ysh[:, c * P:(c + 1) * P], selt[:, :], start=True, stop=False)
                        ins = mm(dst, ysl[:, c * P:(c + 1) * P], selt[:, :], start=False, stop=True)
                    ins.then_inc(scat_done, 1)
            p_last = [False]

            def block_up(i, j):
                s, w = j % BSPLIT, GROUPS[BLOCKS[j][1]] * P
                dst = (H1 if BLOCKS[j][0] == "w1" else H3)[:, 0:w]
                pe.wait_ge(hi_done, i * NB + (UNITS + j + 1))
                for c in range(KC):
                    mm(dst, xgh[:, c, :], bhi[:, s, c * w:(c + 1) * w], start=c == 0, stop=False)
                    mm(dst, xgl[:, c, :], bhi[:, s, c * w:(c + 1) * w], start=False, stop=False)
                pe.wait_ge(lo_done, i * NB + (UNITS + j + 1))
                for c in range(KC):
                    ins = mm(dst, xgh[:, c, :], blo[:, s, c * w:(c + 1) * w], start=False, stop=c == KC - 1)
                ins.then_inc(unit_done, 1)

            def block_down(i, j):
                s, gr = j % BSPLIT, BLOCKS[j][1]
                pe.wait_ge(fh_done, i * 4 + (FF + gr + 1))
                pe.wait_ge(fl_done, i * 4 + (FF + gr + 1))
                pe.wait_ge(hi_done, i * NB + (UNITS + j + 1))
                for part in range(2):
                    if part:
                        pe.wait_ge(lo_done, i * NB + (UNITS + j + 1))
                    for c in range(GROUPS[gr]):
                        for b in range(2):
                            w = (blo if part else bhi)[:, s, c * D + b * 512:c * D + (b + 1) * 512]
                            for a in ((ith,) if part else (ith, itl)):
                                ins = mm(Y[b][:, :], a[:, gr % 2, c, :], w, start=gr == 0 and c == 0 and a is ith and not part,
                                         stop=gr == 3 and part == 1 and c == GROUPS[gr] - 1, skip_group_check=True)
                ins.then_inc(unit_done, 1)

            def turn(i, gr):
                pe.wait_ge(f32_done, i * 4 + (FF + gr + 1))
                pe.wait_ge(fl_done, i * 4 + (FF + gr))
                if gr == 0:
                    pe.wait_ge(st_done, i + 2)
                for c in range(GROUPS[gr]):
                    ins = nc.tensor.transpose(pb[3][:, c * P:(c + 1) * P], inner[:, c * P:(c + 1) * P], ident)
                ins.then_inc(trh_done, 1)

            def moe():
                route()
                pe.wait_ge(tokl_done, 4)
                pe.wait_ge(chosen, 2)
                gather(0)
                n = n_items(pe)
                pe.wait_ge(y_zero, 2)
                with pe.Fori(0, n, 1) as i:
                    for j in range(NB):
                        if j == 0:
                            pe.wait_ge(xgh_done, i * 2 + 2)
                            pe.wait_ge(xgl_done, i * 2 + 2)
                        if j == 11:
                            turn(i, 3)
                            pe.wait_ge(chosen, i * 2 + 4)
                            pe.wait_ge(x_acc, i * 4 + 4)
                            gather(i + 1)
                        if BLOCKS[j][0] == "w1":
                            if j:
                                pe.wait_ge(fs_done, i * 4 + (FF + BLOCKS[j][1]))
                        if BLOCKS[j][0] == "w3":
                            if j > 1:
                                pe.wait_ge(f32_done, i * 4 + (FF + BLOCKS[j][1]))
                        (block_down if BLOCKS[j][0] == "w2" else block_up)(i, j)
                        if j == 1:
                            scatter(i)
                            for t in range(TT):
                                ins = nc.tensor.transpose(pb[3][:, t * P:(t + 1) * P], sel[:, t, :].bitcast(F32), ident)
                            ins.then_inc(str_done, 1)
                        if j in (2, 5, 8):
                            turn(i, (2, 5, 8).index(j))
                p_last[0] = True
                scatter(n)

            norm(0)
            mixer(0)
            norm(1)
            ffn()
            norm(2)
            mixer(1)
            norm(3)
            moe()
            norm(4)


def columns(w):
    kk, n = w.shape
    w = w.reshape(kk // D, KC, P, n // P, P)
    return w.transpose(3, 0, 2, 1, 4).reshape(-1, P, UNIT)


def wide(w):
    w = w.reshape(4, 2, P, w.shape[1] // 512, 512)
    return w.transpose(3, 0, 2, 1, 4).reshape(-1, P, UNIT)


def kernel(**inputs):
    import concourse.bacc as bacc
    from concourse.bass_utils import run_bass_kernel_spmd as run

    a = {n: np.asarray(v) for n, v in inputs.items()}

    def pairs(u, w):
        return np.stack([u, w], 1).reshape(-1, P, UNIT)

    wts = np.empty((UNITS, P, UNIT), np.float32)
    for l in range(DEPTH):
        U = LAYER0[l]
        w_in = a["w_in"][l]
        cut = np.cumsum([0, D, D, VW, VW, D, D, D, D])
        wq, wk, wv, wg, wval, wgate, wga, wgb = (w_in[:, cut[i]:cut[i + 1]] for i in range(8))
        wts[U + GLU0:U + QK0] = pairs(columns(wval), columns(wgate))
        wts[U + QK0:U + V0] = np.concatenate([columns(wq), columns(wk)])
        wts[U + V0:U + G0] = wide(wv)
        wts[U + G0:U + MG0] = columns(wg)
        wts[U + MG0:U + RO0] = pairs(columns(wga), columns(wgb))
        wts[U + RO0:U + CO0] = columns(a["w_ret_o"][l])
        wts[U + CO0:U + WO0] = columns(a["w_conv_o"][l])
        wts[U + WO0:U + MIXER_UNITS] = columns(a["w_out"][l])
        if l == 0:
            f = np.arange(DENSE_CHUNKS)
            at = U + MIXER_UNITS
            wts[at + 3 * f - (f > 0)] = columns(a["dense_w1"][0])
            wts[at + 3 * f + 1 - (f > 0)] = columns(a["dense_w3"][0])
            wts[at + 3 * (f + 1) + 1 - 2 * (f == DENSE_CHUNKS - 1)] = a["dense_w2"][0].reshape(-1, P, UNIT)
    big = np.empty((NEXP, len(BIG_OF), P, BIG), np.float32)
    last_group = np.empty((NEXP, len(LAST_OF), P, LAST), np.float32)
    for b in BLOCKS:
        n0, w = sum(GROUPS[:b[1]]) * P, GROUPS[b[1]] * P
        m = a["moe_" + b[0]][0]
        if b[0] == "w2":
            m = m[:, n0:n0 + w].reshape(NEXP, w // P, P, D)
        else:
            m = m[:, :, n0:n0 + w].reshape(NEXP, KC, P, w)
        m = m.transpose(0, 2, 1, 3).reshape(NEXP, P, -1)
        if b[1] < 3:
            big[:, BIG_OF[b]] = m
        else:
            last_group[:, LAST_OF[b]] = m

    con = np.zeros((P, C_END), np.float32)
    half = QKD // 2
    inv_freq = np.float32(10000.0) ** (-np.arange(half, dtype=np.float32) / np.float32(half))
    ang = (np.arange(T, dtype=np.float32)[None, :] * inv_freq[:, None]).astype(np.float32)
    con[:, C_COS:C_COS + 2 * T] = np.tile(np.cos(ang), 2)
    con[:, C_SIN:C_SIN + 2 * T] = np.tile(np.sin(ang), 2)
    log_g = np.log1p(-np.exp2(-5.0 - np.arange(HEADS)))
    n, m = np.arange(T)[None, :], np.arange(T)[:, None]
    seen = n // CHUNK >= m // CHUNK
    for h in range(HEADS):
        dec = np.where(seen, np.exp(log_g[h] * np.abs(n - m)), 0.0) * QKD ** -0.5
        at = C_DEC + h * SCW
        con[:, at:at + T] = dec[0:P]
        con[:, at + T:at + SCW] = dec[P:, P:]
    con[:, C_IDENT:C_IDENT + P] = np.eye(P)
    con[:, C_ONES:C_ONES + P] = 1.0
    con[:, C_CW:C_VEC] = a["conv_w"].reshape(DEPTH, TAPS, KC, P).transpose(3, 0, 2, 1).reshape(P, -1)
    bg = a["b_gate"]
    vecs = [a["mix_norm"], a["conv_b"], a["conv_ln_g"], a["conv_ln_b"], bg[:, :D], bg[:, D:], a["b_conv_o"], a["ffn_norm"]]
    for i, w in enumerate(vecs):
        for l in range(DEPTH):
            at = C_VEC + (l * len(VECS) + i) * KC
            con[:, at:at + KC] = w[l].reshape(KC, P).T
    con[:, C_FIN:C_FIN + KC] = a["final_norm"].reshape(KC, P).T
    con[:, C_ROUT:C_SM] = a["moe_router"][0].reshape(KC, P, NEXP).transpose(1, 0, 2).reshape(P, -1)
    con[:, C_SM] = 1.0 / D
    con[:, C_SM + 1] = 1.0 / VD
    con[:, C_SM + 2] = EPS
    con[:, C_SM + 3:C_TRI] = np.arange(NEXP)
    con[:, C_TRI:C_IOTA] = np.triu(np.ones((P, P)), 1)
    con[:, C_IOTA:C_END] = np.arange(P)
    xt = np.ascontiguousarray(a["x"].reshape(T, KC, P).transpose(2, 1, 0))

    nc = bacc.Bacc("TRN2", target_bir_lowering=False, num_devices=1)
    feeds = {"xt": xt, "wts": wts, "big": big, "last_group": last_group, "consts": con}
    args = [nc.dram_tensor(n, v.shape, F32, kind="ExternalInput").ap() for n, v in feeds.items()]
    args.append(nc.dram_tensor("out", (P, KC, T), F32, kind="ExternalOutput").ap())
    build(nc, *args)
    r = run(nc, [feeds], core_ids=[0])
    return np.asarray(r.results[0]["out"]).transpose(2, 1, 0).reshape(1, T, D)
```

```python
from contextlib import ExitStack

import numpy as np

import concourse.bass as bass
from concourse import mybir

P = 128
D = 1024
T = 256
DEPTH = 2
KC = D // P
TT = T // P
HEADS = 4
QKD = D // HEADS
VW = 2 * D
VD = VW // HEADS
VC = VW // P
CHUNK = 64
TAPS = 31
PAD = TAPS - 1
DFF = 2816
NEXP = 8
EFF = 1408
EPS = 1e-6

UNIT = 8 * P
RING = 4
GLU_TAPS = (0, 3, 6, 6, 6, 6, 6, 6)
QK_TAPS = 2
V_TAPS = (4, 4, 4, 4)
SCORE_TAPS = 8
G_TAPS = (5, 4)
MG_TAPS = (5, 4, 5, 4, 4, 4, 4, 4, 4, 1, 1, 1, 1, 1, 1, 1)
RO_TAPS = (1, 3, 3, 3)
WARM_START, WARM_END, WARM_SLOTS = 20, 10, 8
WARM_ROUTER = {"first": 4, "sum": 2, "root": 3, "rows": 3}
LN_MEAN, LN_CENTER, LN_VAR = 2, 4, 8
N_GLU, N_QK, N_V, N_G, N_MG, N_RO, N_CO, N_WO = 16, 16, 16, 16, 16, 16, 8, 8
GLU0 = 0
QK0 = GLU0 + N_GLU
V0 = QK0 + N_QK
G0 = V0 + N_V
MG0 = G0 + N_G
RO0 = MG0 + N_MG
TAIL0 = RO0 + N_RO
TAIL = [("co", 0), ("co", 1), ("co", 2)] + [u for c in range(N_CO - 3) for u in (("wo", c), ("co", c + 3))] + \
    [("wo", 5), ("wo", 6), ("wo", 7)]
MIXER_UNITS = TAIL0 + N_CO + N_WO
DENSE_CHUNKS = DFF // P
LAYER0 = (0, MIXER_UNITS + 3 * DENSE_CHUNKS)
UNITS = LAYER0[1] + MIXER_UNITS
STAGE_END = (MIXER_UNITS, LAYER0[1], UNITS)

ITEMS_MOST = NEXP + (2 * T) // (P + 1)
GROUPS = (3, 3, 3, 2)
assert sum(GROUPS) * P == EFF
BLOCKS = (("w1", 0), ("w3", 0), ("w1", 1), ("w3", 1), ("w2", 0), ("w1", 2), ("w3", 2), ("w2", 1),
          ("w1", 3), ("w3", 3), ("w2", 2), ("w2", 3))
NB = len(BLOCKS)
TURN_AFTER = (2, 4, 7, 10)
BIG = max(GROUPS) * D
LAST = min(GROUPS) * D
BIG_OF = {b: i for i, b in enumerate(b for b in BLOCKS if b[1] < 3)}
LAST_OF = {b: i for i, b in enumerate(b for b in BLOCKS if b[1] == 3)}
CHOSE_AT = 12
BRAW, BSPLIT = 4, 3

F32 = mybir.dt.float32
F32R = mybir.dt.float32r
U32 = mybir.dt.uint32
ALU = mybir.AluOpType
ACT = mybir.ActivationFunctionType

FFN_TURN = 4
FFN_TURNS = 4
FFN_UNITS = 3 * FFN_TURN
assert FFN_UNITS % RING == 0

SCW = T + P
C_IDENT = 0
C_VEC = C_IDENT + P
VECS = ("mix", "convb", "lng", "lnb", "bga", "bgb", "bco", "ffn")
C_FIN = C_VEC + DEPTH * len(VECS) * KC
C_SM = C_FIN + KC
C_LATER = C_SM + 3 + NEXP
C_ONES = C_LATER
C_CW = C_ONES + P
C_ROUT = C_CW + DEPTH * KC * TAPS
C_TRI = C_ROUT + KC * NEXP
C_IOTA = C_TRI + P
C_COS = C_IOTA + P
C_SIN = C_COS + 2 * T
C_DEC = C_SIN + 2 * T
C_END = C_DEC + HEADS * SCW


def build(nc, xt, wts, big, last_group, consts, out):
    with ExitStack() as ctx:
        def sem(name):
            return ctx.enter_context(nc.semaphore(name))

        base = [nc.sbuf_base + (-nc.sbuf_base) % 64]
        places = {}

        def sb(name, shape, dt=F32, over=None, skip=0):
            size = 4 * int(np.prod(shape[1:]))
            if over is None:
                at = base[0]
                base[0] += size + (-size) % 64
                places[name] = (at, size)
            else:
                at, room = places[over]
                at += skip
                assert skip + size <= room, name
            return nc.alloc_sbuf_tensor_at(name, shape, dt, offset=at)

        x = sb("x", [P, KC, T])
        hnh = sb("hnh", [P, KC, T], F32R)
        hnl = sb("hnl", [P, KC, T], F32R)
        raw = sb("raw", [P, RING, UNIT])
        whi = sb("whi", [P, RING, UNIT], F32R)
        wlo = sb("wlo", [P, RING, UNIT], F32R)
        prob = sb("prob", [P, HEADS, SCW])
        rsq = sb("rsq", [P, 2, 4, T])
        q = sb("q", [P, HEADS, 2 * T])
        k = sb("k", [P, HEADS, 2 * T])
        v = sb("v", [P, HEADS, TT, VD])
        rh = sb("rh", [P, VC, T], F32R)
        g = sb("g", [P, VC, T])
        mga = sb("mga", [P, KC, T])
        mgb = sb("mgb", [P, KC, T])
        up = sb("up", [P, KC, PAD + T])
        cv = sb("cv", [P, KC, T])
        con = sb("con", [P, C_END])
        mtmp = sb("mtmp", [P, 2, T])
        itl = sb("itl", [P, 2, 3, P], F32R)
        small = sb("small", [P, 256])
        uh = sb("uh", [P, KC, T], F32R, over="q")
        ul = sb("ul", [P, KC, T], F32R, over="k")
        rl = sb("rl", [P, VC, T], F32R, over="v")
        mh = sb("mh", [P, KC, T], F32R, over="g")
        ml = sb("ml", [P, KC, T], F32R, over="g", skip=4 * KC * T)
        gated = sb("gated", [P, KC, T], F32, over="rsq")
        sig = sb("sig", [P, 2, T], F32, over="rh")
        root = sb("root", [P, T], F32, over="mtmp")
        inv = sb("inv", [P, T], F32, over="mtmp", skip=4 * T)
        xsum = sb("xsum", [P, 4, T], F32, over="rsq")
        lsum = sb("lsum", [P, 4, T], F32, over="up")
        rot = sb("rot", [P, 2, 2, 2 * T], F32, over="rh", skip=8 * T)
        xsq = sb("xsq", [P, KC, T], F32, over="mga")
        hn32 = sb("hn32", [P, KC, T], F32, over="mgb")
        lnsq = sb("lnsq", [P, KC, T], F32, over="q")
        yout = sb("yout", [P, KC, T], F32, over="cv")
        fs = sb("fs", [P, 2, T], F32, over="mga")
        f32_ = sb("f32_", [P, 2, T], F32, over="mga", skip=8 * T)
        fhh = sb("fhh", [P, 4, T], F32R, over="g")
        fhl = sb("fhl", [P, 4, T], F32R, over="g", skip=16 * T)
        def across(first, size):
            places[first + "+"] = (places[first][0], size)
            return first + "+"
        split_room = across("hnh", 2 * 4 * BSPLIT * BIG)
        assert places["hnh"][0] + places[split_room][1] <= places["q"][0]
        bhi = sb("bhi", [P, BSPLIT, BIG], F32R, over=split_room)
        blo = sb("blo", [P, BSPLIT, BIG], F32R, over=split_room, skip=4 * BSPLIT * BIG)
        assert places["q"][0] + 4 * BRAW * BIG <= places["g"][0]
        braw = sb("braw", [P, BRAW, BIG], F32, over=across("q", 4 * BRAW * BIG))
        hth = sb("hth", [P, TT, D], F32R, over="g")
        htl = sb("htl", [P, TT, D], F32R, over="g", skip=4 * TT * D)
        xgh = sb("xgh", [P, KC, P], F32R, over="mga")
        xgl = sb("xgl", [P, KC, P], F32R, over="mga", skip=4 * KC * P)
        ysh = sb("ysh", [P, D], F32R, over="cv")
        ysl = sb("ysl", [P, D], F32R, over="cv", skip=4 * D)
        act3 = sb("act3", [P, 3 * P], F32, over="up")
        inner = sb("inner", [P, 3 * P], F32, over="up", skip=12 * P)
        sel = sb("sel", [P, TT, P], F32R, over="up", skip=24 * P)
        selt = sb("selt", [P, T], F32R, over="up", skip=32 * P)
        ith = sb("ith", [P, 2, 3, P], F32R, over="up", skip=40 * P)
        assert base[0] <= nc.sbuf_usable_end, base[0]

        pa = [ctx.enter_context(nc.psum_tensor(f"pa{i}", [P, 512], F32)) for i in range(4)]
        pb = [ctx.enter_context(nc.psum_tensor(f"pb{i}", [P, 512], F32)) for i in range(4)]

        cos2, sin2 = con[:, C_COS:C_COS + 2 * T], con[:, C_SIN:C_SIN + 2 * T]
        ident, ones = con[:, C_IDENT:C_IDENT + P], con[:, C_ONES:C_ONES + P]
        inv_d, inv_v, eps = (con[:, C_SM + i:C_SM + i + 1] for i in range(3))
        mean_of = con[:, C_SM:C_SM + 1].broadcast_to([P, P])
        expert_no = con[:, C_SM + 3:C_SM + 3 + NEXP]
        before = con[:, C_TRI:C_TRI + P]
        slot_no = con[:, C_IOTA:C_IOTA + P]
        slot_of = small[:, 128:128 + 2 * 12].rearrange("p (i t) -> p i t", t=TT)
        gate_of = small[:, 152:152 + 2 * 12].rearrange("p (i t) -> p i t", t=TT)
        slot_gate = small[:, 176:177]
        plan = small[:, 180:184].bitcast(mybir.dt.int32)

        def vec(l, what, c):
            at = C_VEC + (l * len(VECS) + VECS.index(what)) * KC + c
            return con[:, at:at + 1]

        def tap(l, c, t):
            at = C_CW + (l * KC + c) * TAPS + t
            return con[:, at:at + 1]

        landed = [sem(f"landed{i}") for i in range(RING)]
        con_in, con2_in, out_done = sem("con_in"), sem("con2_in"), sem("out_done")
        x_in = [sem(f"x_in{c}") for c in range(4)]
        hi_done, lo_done, unit_done = sem("hi_done"), sem("lo_done"), sem("unit_done")
        pad_zero, warm_zero = sem("pad_zero"), sem("warm_zero")
        sq_done, sum_done = sem("sq_done"), sem("sum_done")
        stat_done, rms_done, inv_done, bc_done = (sem(n) for n in ("stat_done", "rms_done", "inv_done", "bc_done"))
        n32_done, nh_done, nl_done = sem("n32_done"), sem("nh_done"), sem("nl_done")
        acc_done = sem("acc_done")
        x_done = sem("x_done")
        sig_done, u_done = sem("sig_done"), sem("u_done")
        tap0, conv = sem("tap0"), sem("conv")
        rot_step, qk_done = sem("rot_step"), sem("qk_done")
        v_done = sem("v_done")
        score_done, prob_done = sem("score_done"), sem("prob_done")
        g_done, pv_done, rsq_done, rg_done = sem("g_done"), sem("pv_done"), sem("rsq_done"), sem("rg_done")
        rsum_done, rstat_done, rrms_done, rinv_done, rbc_done = (sem(n) for n in (
            "rsum_done", "rstat_done", "rrms_done", "rinv_done", "rbc_done"))
        rn_done, rh_done, rl_done = sem("rn_done"), sem("rh_done"), sem("rl_done")
        mg_done = sem("mg_done")
        lsum1, lmean, lcen = sem("lsum1"), sem("lmean"), sem("lcen")
        lsq, lsum2, lstat, lrms, linv, lnrm = (sem(n) for n in ("lsq", "lsum2", "lstat", "lrms", "linv", "lnrm"))
        lact, uh_done, ul_done = sem("lact"), sem("uh_done"), sem("ul_done")
        gated_done, mstep, mh_done, ml_done = sem("gated_done"), sem("mstep"), sem("mh_done"), sem("ml_done")
        fs_done, f32_done, fh_done, fl_done = sem("fs_done"), sem("f32_done"), sem("fh_done"), sem("fl_done")
        blanded = [sem(f"blanded{i}") for i in range(BRAW)]
        logit_done, top, ex_done = sem("logit_done"), sem("top"), sem("ex_done")
        tok_tr, tokh_done, tokl_done = sem("tok_tr"), sem("tokh_done"), sem("tokl_done")
        pos_done, plan_done = sem("pos_done"), sem("plan_done")
        chosen, gath_done = sem("chosen"), sem("gath_done")
        xgh_done, xgl_done = sem("xgh_done"), sem("xgl_done")
        str_done, st_done, trh_done = sem("str_done"), sem("st_done"), sem("trh_done")
        yh_done, yl_done, scat_done, x_acc = sem("yh_done"), sem("yl_done"), sem("scat_done"), sem("x_acc")
        fin_done = sem("fin_done")

        block = ctx.enter_context(nc.Block())

        FF = DENSE_CHUNKS
        H1, H3, Y = pa[0], pa[1], pa[2:4]
        TOK = (pb[0], pb[1], pb[3], pa[1])
        SCAT = (pb[0], pb[1], pb[2], Y[0])

        def block_source(e, j):
            b = BLOCKS[j]
            if b[1] < 3:
                return big[e, BIG_OF[b]], BIG
            return last_group[e, LAST_OF[b]], LAST

        def cols(j):
            return GROUPS[BLOCKS[j][1]] * D

        def at(count, i=None, step=0):
            return count if i is None else i * step + count

        def n_items(eng):
            eng.wait_ge(plan_done, 1)
            return eng.value_load(plan[0:1, 0:1], min_val=NEXP, max_val=ITEMS_MOST)

        @block.sync
        def _(sp):
            for c in range(4):
                sp.dma_start(x[:, 2 * c:2 * c + 2, :], xt[:, 2 * c:2 * c + 2, :]).then_inc(x_in[c], 16)
            sp.dma_start(con[:, 0:C_LATER], consts[:, 0:C_LATER]).then_inc(con_in, 16)

            def load(u, slot):
                sp.dma_start(raw[:, slot, :], wts[u]).then_inc(landed[slot], 16)
            for s in range(RING):
                load(s, s)
            sp.dma_start(con[:, C_LATER:C_END], consts[:, C_LATER:C_END]).then_inc(con2_in, 16)
            n = UNITS // RING - 1
            with sp.Fori(0, n, 1) as it:
                for s in range(RING):
                    sp.wait_ge(lo_done, it * RING + (s + 1))
                    load(bass.ds(it * RING + (RING + s), 1), s)
            for s in range(UNITS % RING):
                sp.wait_ge(lo_done, n * RING + s + 1)
                load((n + 1) * RING + s, s)
            sp.wait_ge(unit_done, LAYER0[1] + TAIL0 + TAIL.index(("co", N_CO - 1)) + 1)

            def load_item(i, e):
                for j in range(NB):
                    sp.wait_ge(lo_done, i * NB + (UNITS + j - BRAW + 1))
                    src, w = block_source(e, j)
                    sp.dma_start(braw[:, j % BRAW, 0:w], src).then_inc(blanded[j % BRAW], 16)
            with sp.Fori(0, NEXP, 1) as e:
                load_item(e, bass.ds(e, 1))
            n = n_items(sp)
            with sp.If(n > NEXP):
                with sp.Fori(NEXP, n, 1) as i:
                    e = sp.value_load(plan[0:1, bass.ds(i - (NEXP - 1), 1)], min_val=0, max_val=NEXP - 1)
                    load_item(i, bass.ds(e, 1))
            for j in range(BSPLIT - 1):
                sp.wait_ge(lo_done, n * NB + (UNITS + j - BRAW + 1))
                sp.sem_inc(blanded[j % BRAW], 16)
            for c in range(4):
                sp.wait_ge(fin_done, c + 1)
                sp.dma_start(out[:, 2 * c:2 * c + 2, :], yout[:, 2 * c:2 * c + 2, :]).then_inc(out_done, 16)
            sp.wait_ge(out_done, 4 * 16)

        @block.gpsimd
        def _(pool):
            nc.gpsimd.memset(mtmp[:, :, :], 0.0).then_inc(warm_zero, 1)
            nc.gpsimd.memset(up[:, :, 0:PAD], 0.0).then_inc(pad_zero, 1)
            pool.wait_ge(lact, KC)
            nc.gpsimd.memset(up[:, :, 0:PAD], 0.0).then_inc(pad_zero, 1)
            pool.wait_ge(x_done, 12)
            nc.gpsimd.memset(ysh[:, :].bitcast(F32), 0.0).then_inc(yh_done, 2)
            nc.gpsimd.memset(ysl[:, :].bitcast(F32), 0.0).then_inc(yl_done, 2)
            nc.gpsimd.memset(selt[:, :].bitcast(F32), 0.0).then_inc(st_done, 1)

        @block.scalar
        def _(act):
            def split_hi(u, i=None):
                if u >= UNITS:
                    return
                act.wait_ge(landed[u % RING], at(16 * (u // RING + 1), i, 16 * FFN_UNITS // RING))
                if u >= RING:
                    act.wait_ge(unit_done, at(u - RING + 1, i, FFN_UNITS))
                nc.scalar.copy(whi[:, u % RING, :], raw[:, u % RING, :]).then_inc(hi_done, 1)

            def load_root_table():
                nc.scalar.activation(small[:, 0:1], eps, ACT.Sqrt)

            def norm(n):
                for c in range(4):
                    if n == 0:
                        act.wait_ge(x_in[c], 16)
                    else:
                        act.wait_ge(x_done, 4 * (n - 1) + c + 1)
                    nc.scalar.activation(xsq[:, 2 * c:2 * c + 2, :], x[:, 2 * c:2 * c + 2, :],
                                         ACT.Square).then_inc(sq_done, 1)
                if n == 0:
                    act.wait_ge(con_in, 16)
                if 1 <= n <= len(STAGE_END):
                    split_hi(STAGE_END[n - 1] + 3)
                if n == 0:
                    split_hi(0)
                act.wait_ge(stat_done, n + 1)
                nc.scalar.activation(small[:, 2:2 + TT], pa[0][:, 0:TT], ACT.Sqrt, bias=eps).then_inc(rms_done, 1)
                if n >= 2 * DEPTH - 1:
                    return
                for c in range(KC):
                    if n == 0 and c == 0:
                        split_hi(1)
                        split_hi(2)
                    if n == 0 and c == 4:
                        split_hi(3)
                    act.wait_ge(n32_done, 8 * n + c + 1)
                    nc.scalar.copy(hnh[:, c, :], hn32[:, c, :]).then_inc(nh_done, 1)

            def mixer(l):
                U = LAYER0[l]

                def first_tap(c):
                    if l == 0 and c == 0:
                        act.wait_ge(con2_in, 16)
                    act.wait_ge(u_done, 8 * l + c + 1)
                    nc.scalar.activation(cv[:, c, :], up[:, c, 0:T], ACT.Identity, bias=vec(l, "convb", c),
                                         scale=tap(l, c, 0)).then_inc(tap0, 1)
                for p in range(8):
                    split_hi(U + GLU0 + 2 * p + 4)
                    act.wait_ge(unit_done, U + GLU0 + 2 * p + 2)
                    if 8 * l + p >= 2:
                        act.wait_ge(u_done, 8 * l + p - 1)
                    nc.scalar.activation(sig[:, p % 2, :], pa[p % 4][:, T:2 * T], ACT.Sigmoid).then_inc(sig_done, 1)
                    split_hi(U + GLU0 + 2 * p + 5)
                    if p:
                        first_tap(p - 1)
                for j in range(N_QK):
                    split_hi(U + QK0 + j + 4)
                    if j == 0:
                        first_tap(7)
                for cg in range(4):
                    for j in range(3):
                        split_hi(U + V0 + 4 * cg + j + 4)
                    act.wait_ge(unit_done, U + V0 + 4 * cg + 4)
                    for t in range(TT):
                        nc.scalar.copy(v[:, cg, t, :], pa[(2 * cg + t) % 4][:, :]).then_inc(v_done, 1)
                    split_hi(U + V0 + 4 * cg + 7)

                def squares(h):
                    act.wait_ge(pv_done, 4 * l + h + 1)
                    if 4 * l + h >= 2:
                        act.wait_ge(rstat_done, 4 * l + h - 1)
                    for b in range(2):
                        nc.scalar.activation(rsq[:, h % 2, 2 * b:2 * b + 2, :], pb[b][:, :],
                                             ACT.Square).then_inc(rsq_done, 1)
                for p in range(8):
                    split_hi(U + G0 + 2 * p + 4)
                    act.wait_ge(unit_done, U + G0 + 2 * p + 2)
                    nc.scalar.activation(g[:, 2 * p:2 * p + 2, :], pa[p % 4][:, :], ACT.Silu).then_inc(g_done, 1)
                    if p in (2, 4, 6):
                        squares((p - 2) // 2)
                    split_hi(U + G0 + 2 * p + 5)

                def ret_hi(h):
                    act.wait_ge(rn_done, 4 * l + h + 1)
                    nc.scalar.copy(rh[:, 4 * h:4 * h + 4, :], g[:, 4 * h:4 * h + 4, :]).then_inc(rh_done, 1)
                for p in range(8):
                    split_hi(U + MG0 + 2 * p + 4)
                    act.wait_ge(unit_done, U + MG0 + 2 * p + 2)
                    nc.scalar.activation(mga[:, p, :], pa[p % 4][:, 0:T], ACT.Sigmoid, bias=vec(l, "bga", p))
                    nc.scalar.activation(mgb[:, p, :], pa[p % 4][:, T:2 * T], ACT.Sigmoid,
                                         bias=vec(l, "bgb", p)).then_inc(mg_done, 1)
                    split_hi(U + MG0 + 2 * p + 5)
                    if p == 0:
                        squares(3)
                    if p == 2:
                        act.wait_ge(rstat_done, 4 * l + 4)
                        nc.scalar.activation(small[:, 8:16], pb[2][:, 8:16], ACT.Sqrt, bias=eps).then_inc(rrms_done, 1)
                    if p >= 4:
                        ret_hi(p - 4)
                for j in range(N_RO):
                    split_hi(U + RO0 + j + 4)
                    if j == LN_CENTER:
                        for c in range(4):
                            act.wait_ge(lcen, 8 * l + 2 * c + 2)
                            nc.scalar.activation(lnsq[:, 2 * c:2 * c + 2, :], cv[:, 2 * c:2 * c + 2, :],
                                                 ACT.Square).then_inc(lsq, 1)
                    if j == LN_VAR:
                        act.wait_ge(lstat, l + 1)
                        nc.scalar.activation(root[:, :], pb[3][:, 0:T], ACT.Sqrt, bias=eps).then_inc(lrms, 1)
                    if LN_VAR < j <= LN_VAR + 4:
                        c = j - LN_VAR - 1
                        for cc in (2 * c, 2 * c + 1):
                            act.wait_ge(lnrm, 8 * l + cc + 1)
                            nc.scalar.activation(cv[:, cc, :], cv[:, cc, :], ACT.Silu, bias=vec(l, "lnb", cc),
                                                 scale=vec(l, "lng", cc)).then_inc(lact, 1)
                        act.wait_ge(lact, 8 * l + 2 * c + 2)
                        nc.scalar.copy(uh[:, 2 * c:2 * c + 2, :], cv[:, 2 * c:2 * c + 2, :]).then_inc(uh_done, 1)
                load_root_table()
                for n, (what, c) in enumerate(TAIL):
                    if n < len(TAIL) - 1:
                        split_hi(U + TAIL0 + n + 4)
                    if what == "co":
                        act.wait_ge(mstep, 3 * (8 * l + c) + 3)
                        nc.scalar.copy(mh[:, c, :], cv[:, c, :]).then_inc(mh_done, 1)

            def ffn():
                U, F = MIXER_UNITS, DENSE_CHUNKS

                def chunk(f, i=None):
                    split_hi(U + 3 * f + 3 + (f == 0), i)
                    act.wait_ge(unit_done, at(U + 3 * f + 1 + (f == 0), i, FFN_UNITS))
                    if f >= 2:
                        act.wait_ge(f32_done, at(f - 1, i, FFN_TURN))
                    nc.scalar.activation(fs[:, f % 2, :], pa[f % 4][:, 0:T], ACT.Silu).then_inc(fs_done, 1)
                    if f:
                        split_hi(U + 3 * f + 4, i)
                    act.wait_ge(f32_done, at(f + 1, i, FFN_TURN))
                    if f >= 4 or i is not None:
                        act.wait_ge(unit_done, at(U + 3 * (f - 4) + 5, i, FFN_UNITS))
                    nc.scalar.copy(fhh[:, f % 4, :], f32_[:, f % 2, :]).then_inc(fh_done, 1)
                    if f == F - 1:
                        load_root_table()
                    split_hi(U + 3 * f + 5, i)
                for f in range(2):
                    chunk(f)
                with act.Fori(0, FFN_TURNS, 1) as i:
                    for f in range(2, 2 + FFN_TURN):
                        chunk(f, i)
                for f in range(2 + FFN_TURN * FFN_TURNS, F):
                    chunk(f)

            def split_block(i, j):
                act.wait_ge(blanded[j % BRAW], i * (16 * NB // BRAW) + 16 * (j // BRAW + 1))
                act.wait_ge(unit_done, i * NB + (UNITS + j - BSPLIT + 1))
                w = cols(j % NB)
                nc.scalar.copy(bhi[:, j % BSPLIT, 0:w], braw[:, j % BRAW, 0:w]).then_inc(hi_done, 1)

            def tokens():
                for b in range(4):
                    act.wait_ge(tok_tr, b // 2 + 1)
                    nc.scalar.copy(hth[:, b % 2, (b // 2) * 512:(b // 2) * 512 + 512], TOK[b][:, :]).then_inc(tokh_done, 1)

            def rows(i):
                act.wait_ge(gath_done, i + 1)
                nc.scalar.copy(slot_gate, pb[2][:, 0:1])
                for b in range(2):
                    nc.scalar.copy(xgh[:, 4 * b:4 * b + 4, :], pb[b][:, :]).then_inc(xgh_done, 1)

            def outputs(i):
                act.wait_ge(unit_done, i * NB + UNITS)
                for b in range(2):
                    nc.scalar.copy(ysh[:, b * 512:(b + 1) * 512], Y[b][:, :]).then_inc(yh_done, 1)

            def moe():
                for j in range(BSPLIT - 1):
                    split_block(0, j)
                nc.scalar.activation(small[:, 0:1], eps, ACT.Exp)
                tokens()
                act.wait_ge(top, 4)
                nc.scalar.activation(small[:, 80:80 + TT], small[:, 76:76 + TT], ACT.Exp).then_inc(ex_done, 1)
                rows(0)
                nc.scalar.activation(small[:, 0:1], eps, ACT.Silu)
                n = n_items(act)
                with act.Fori(0, n, 1) as i:
                    split_block(i, BSPLIT - 1)
                    for j in range(NB):
                        if BLOCKS[j][0] == "w1":
                            gr = BLOCKS[j][1]
                            w = GROUPS[gr] * P
                            act.wait_ge(unit_done, i * NB + (UNITS + j + 1))
                            act.wait_ge(f32_done, i * 4 + (FF + gr))
                            nc.scalar.activation(act3[:, 0:w], H1[:, 0:w], ACT.Silu).then_inc(fs_done, 1)
                        if j in TURN_AFTER:
                            gr = TURN_AFTER.index(j)
                            w = GROUPS[gr]
                            act.wait_ge(trh_done, i * 4 + (gr + 1))
                            nc.scalar.copy(ith[:, gr % 2, 0:w, :], pb[3][:, 0:w * P]).then_inc(fh_done, 1)
                        if j == NB - 1:
                            outputs(i + 1)
                        else:
                            split_block(i, j + BSPLIT)
                        if j == 10:
                            rows(i + 1)
                        if j == 1:
                            act.wait_ge(str_done, i + 1)
                            nc.scalar.copy(selt[:, :], pb[3][:, 0:T]).then_inc(st_done, 1)

            norm(0)
            mixer(0)
            norm(1)
            ffn()
            norm(2)
            mixer(1)
            norm(3)
            moe()
            norm(4)

        @block.vector
        def _(dve):
            def split_lo(u, i=None):
                if u >= UNITS:
                    return
                dve.wait_ge(hi_done, at(u + 1, i, FFN_UNITS))
                if u >= RING:
                    dve.wait_ge(unit_done, at(u - RING + 1, i, FFN_UNITS))
                nc.vector.tensor_tensor(wlo[:, u % RING, :], raw[:, u % RING, :],
                                        whi[:, u % RING, :].bitcast(F32), ALU.subtract).then_inc(lo_done, 1)

            def conv_ops(l, first, last):
                taps = TAPS - 1
                for n in range(first, min(last, KC * taps)):
                    c, t = 2 * (n // (2 * taps)) + n % 2, (n % (2 * taps)) // 2 + 1
                    if t == 1:
                        dve.wait_ge(tap0, KC * l + c + 1)
                    else:
                        dve.wait_ge(conv, l * KC * taps + n - 1)
                    nc.vector.scalar_tensor_tensor(out=cv[:, c, :], in0=up[:, c, t:t + T], scalar=tap(l, c, t),
                                                   in1=cv[:, c, :], op0=ALU.mult, op1=ALU.add).then_inc(conv, 1)

            def square_sum(n, c):
                dve.wait_ge(sq_done, 4 * n + c + 1)
                nc.vector.tensor_tensor(xsum[:, c, :], xsq[:, 2 * c, :], xsq[:, 2 * c + 1, :],
                                        ALU.add).then_inc(sum_done, 1)

            def add_outputs(k, units):
                for p in range(4):
                    if p >= 2:
                        square_sum(k + 1, p - 2)
                    if p < 3:
                        dve.wait_ge(acc_done, 3 * k + p + 1)
                    else:
                        dve.wait_ge(unit_done, units)
                    xx = x[:, 2 * p:2 * p + 2, :]
                    nc.vector.tensor_tensor(xx, pb[p][:, :].rearrange("p (c t) -> p c t", c=2), xx,
                                            ALU.add).then_inc(x_done, 1)

            def norm(n):
                for c in range(4):
                    if n == 0 or c >= 2:
                        square_sum(n, c)
                dve.wait_ge(rms_done, n + 1)
                nc.vector.reciprocal(small[:, 4:4 + TT], small[:, 2:2 + TT]).then_inc(inv_done, 1)
                if n == 0:
                    split_lo(0)
                dve.wait_ge(bc_done, n + 1)
                last = n == 2 * DEPTH
                for c in range(KC):
                    gain = con[:, C_FIN + c:C_FIN + c + 1] if last else vec(n // 2, ("mix", "ffn")[n % 2], c)
                    nc.vector.scalar_tensor_tensor(out=(yout if last else hn32)[:, c, :], in0=x[:, c, :], scalar=gain,
                                                   in1=pa[3][:, 0:T], op0=ALU.mult, op1=ALU.mult).then_inc(
                                                       fin_done if last and c % 2 else n32_done, 1)
                if n >= 2 * DEPTH - 1:
                    return
                for c in range(4):
                    dve.wait_ge(nh_done, 8 * n + 2 * c + 2)
                    nc.vector.tensor_tensor(hnl[:, 2 * c:2 * c + 2, :], hn32[:, 2 * c:2 * c + 2, :],
                                            hnh[:, 2 * c:2 * c + 2, :].bitcast(F32), ALU.subtract).then_inc(nl_done, 1)
                for u in range(2 if n else 1, 4):
                    split_lo(STAGE_END[n - 1] + u if n else u)

            def mixer(l):
                U = LAYER0[l]
                for p in range(8):
                    if l == 0 and p == 2:
                        dve.wait_ge(con2_in, 16)
                    split_lo(U + GLU0 + 2 * p + 4)
                    dve.wait_ge(sig_done, 8 * l + p + 1)
                    if p == 0:
                        dve.wait_ge(pad_zero, l + 1)
                    nc.vector.tensor_tensor(up[:, p, PAD:], pa[p % 4][:, 0:T], sig[:, p % 2, :],
                                            ALU.mult).then_inc(u_done, 1)
                    split_lo(U + GLU0 + 2 * p + 5)
                    done = sum(GLU_TAPS[0:p + 1])
                    conv_ops(l, done - GLU_TAPS[p], done)
                for p in range(8):
                    dst, h = (q, p) if p < 4 else (k, p - 4)
                    split_lo(U + QK0 + 2 * p + 4)
                    dve.wait_ge(unit_done, U + QK0 + 2 * p + 2)
                    if p >= 2 or l:
                        dve.wait_ge(qk_done, 2 * (8 * l + p - 1))
                    nc.vector.tensor_tensor(rot[:, p % 2, 0, :], pa[p % 4][:, :], cos2, ALU.mult).then_inc(rot_step, 1)
                    nc.vector.tensor_tensor(rot[:, p % 2, 1, :], pa[p % 4][:, :], sin2, ALU.mult).then_inc(rot_step, 1)
                    conv_ops(l, done, done + QK_TAPS)
                    split_lo(U + QK0 + 2 * p + 5)
                    dve.wait_ge(rot_step, 2 * (8 * l + p + 1))
                    nc.vector.tensor_tensor(dst[:, h, 0:T], rot[:, p % 2, 0, 0:T], rot[:, p % 2, 1, T:],
                                            ALU.subtract).then_inc(qk_done, 1)
                    nc.vector.tensor_tensor(dst[:, h, T:], rot[:, p % 2, 1, 0:T], rot[:, p % 2, 0, T:],
                                            ALU.add).then_inc(qk_done, 1)
                    done += QK_TAPS
                for j in range(N_V):
                    split_lo(U + V0 + j + 4)
                    conv_ops(l, done, done + V_TAPS[j % 4])
                    done += V_TAPS[j % 4]
                conv_ops(l, done, done + SCORE_TAPS)
                done += SCORE_TAPS
                for h in range(HEADS):
                    dve.wait_ge(score_done, 4 * l + h + 1)
                    nc.vector.tensor_tensor(prob[:, h, :], pb[h][:, 0:SCW], con[:, C_DEC + h * SCW:C_DEC + (h + 1) * SCW],
                                            ALU.mult).then_inc(prob_done, 1)

                def gate_r(h):
                    dve.wait_ge(pv_done, 4 * l + h + 1)
                    dve.wait_ge(g_done, 8 * l + 2 * h + 2)
                    for b in range(2):
                        c = 4 * h + 2 * b
                        dve.wait_ge(rsq_done, 8 * l + 2 * h + b + 1)
                        nc.vector.tensor_tensor(g[:, c:c + 2, :], pb[b][:, :].rearrange("p (c t) -> p c t", c=2),
                                                g[:, c:c + 2, :], ALU.mult).then_inc(rg_done, 1)
                    nc.vector.tensor_tensor(rsq[:, h % 2, 0:2, :], rsq[:, h % 2, 0:2, :], rsq[:, h % 2, 2:4, :],
                                            ALU.add).then_inc(rsum_done, 1)
                for p in range(8):
                    split_lo(U + G0 + 2 * p + 4)
                    conv_ops(l, done, done + G_TAPS[0])
                    done += G_TAPS[0]
                    if p in (2, 4, 6):
                        gate_r((p - 2) // 2)
                    split_lo(U + G0 + 2 * p + 5)
                    conv_ops(l, done, done + G_TAPS[1])
                    done += G_TAPS[1]

                def ret_norm(h):
                    dve.wait_ge(rbc_done, 4 * l + h + 1)
                    bc = pb[h // 2][:, (h % 2) * T:(h % 2) * T + T]
                    nc.vector.tensor_tensor(g[:, 4 * h:4 * h + 4, :], g[:, 4 * h:4 * h + 4, :],
                                            bc.rearrange("p (o t) -> p o t", o=1).broadcast_to([P, 4, T]),
                                            ALU.mult).then_inc(rn_done, 1)

                def ret_lo(h):
                    dve.wait_ge(rh_done, 4 * l + h + 1)
                    nc.vector.tensor_tensor(rl[:, 4 * h:4 * h + 4, :], g[:, 4 * h:4 * h + 4, :],
                                            rh[:, 4 * h:4 * h + 4, :].bitcast(F32), ALU.subtract).then_inc(rl_done, 1)
                for j in range(N_MG):
                    split_lo(U + MG0 + j + 4)
                    if j == 1:
                        gate_r(3)
                    if j == 6:
                        dve.wait_ge(rrms_done, l + 1)
                        nc.vector.reciprocal(small[:, 16:24], small[:, 8:16]).then_inc(rinv_done, 1)
                    if j in (9, 10, 12, 14):
                        ret_norm((9, 10, 12, 14).index(j))
                    if j in (11, 13, 15):
                        ret_lo((j - 11) // 2)
                    conv_ops(l, done, done + MG_TAPS[j])
                    done += MG_TAPS[j]

                def halves(src, done):
                    nc.vector.tensor_tensor(lsum[:, :, :], src[:, 0:4, :], src[:, 4:8, :], ALU.add).then_inc(done, 1)
                    dve.wait_ge(done, 2 * l + 1)
                    nc.vector.tensor_tensor(lsum[:, 0:2, :], lsum[:, 0:2, :], lsum[:, 2:4, :], ALU.add).then_inc(done, 1)
                for j in range(N_RO):
                    c = 2 * (j // 4) + j % 2
                    if j % 4 >= 2:
                        dve.wait_ge(unit_done, U + RO0 + j + 1)
                        if j == 2:
                            dve.wait_ge(mg_done, 8 * l + 8)
                        nc.vector.tensor_tensor(gated[:, c, :], pa[c % 4][:, 0:T],
                                                mga[:, c, :], ALU.mult).then_inc(gated_done, 1)
                    split_lo(U + RO0 + j + 4)
                    if j == 0:
                        ret_lo(3)
                    if j <= LN_MEAN:
                        last = KC * (TAPS - 1) if j == LN_MEAN else done + RO_TAPS[j]
                        conv_ops(l, done, last)
                        done = last
                    if j == LN_MEAN:
                        dve.wait_ge(conv, (l + 1) * KC * (TAPS - 1))
                        halves(cv, lsum1)
                    if j == LN_CENTER:
                        dve.wait_ge(lmean, l + 1)
                        for c in range(KC):
                            nc.vector.tensor_tensor(cv[:, c, :], cv[:, c, :], pb[2][:, 0:T], ALU.subtract).then_inc(lcen, 1)
                    if j == LN_CENTER + 1:
                        dve.wait_ge(lsq, 4 * l + 4)
                        halves(lnsq, lsum2)
                    if j == LN_VAR:
                        dve.wait_ge(lrms, l + 1)
                        nc.vector.reciprocal(inv[:, :], root[:, :]).then_inc(linv, 1)
                        dve.wait_ge(linv, l + 1)
                        for c in range(KC):
                            nc.vector.tensor_tensor(cv[:, c, :], cv[:, c, :], inv[:, :], ALU.mult).then_inc(lnrm, 1)
                    if LN_VAR + 1 < j <= LN_VAR + 5:
                        c = j - LN_VAR - 2
                        dve.wait_ge(uh_done, 4 * l + c + 1)
                        nc.vector.tensor_tensor(ul[:, 2 * c:2 * c + 2, :], cv[:, 2 * c:2 * c + 2, :],
                                                uh[:, 2 * c:2 * c + 2, :].bitcast(F32), ALU.subtract).then_inc(ul_done, 1)
                for n, (what, c) in enumerate(TAIL):
                    if what == "co":
                        m = 3 * (8 * l + c)
                        dve.wait_ge(unit_done, U + TAIL0 + n + 1)
                        nc.vector.scalar_tensor_tensor(out=mtmp[:, c % 2, :], in0=pa[c % 4][:, 0:T],
                                                       scalar=vec(l, "bco", c), in1=mgb[:, c, :], op0=ALU.add,
                                                       op1=ALU.mult).then_inc(mstep, 1)
                        dve.wait_ge(ul_done, 4 * l + 4)
                        dve.wait_ge(mstep, m + 1)
                        nc.vector.tensor_tensor(cv[:, c, :], mtmp[:, c % 2, :], gated[:, c, :], ALU.add).then_inc(mstep, 2)
                    if n < len(TAIL) - 2:
                        split_lo(U + TAIL0 + n + 4)
                    if what == "co":
                        dve.wait_ge(mh_done, 8 * l + c + 1)
                        nc.vector.tensor_tensor(ml[:, c, :], cv[:, c, :], mh[:, c, :].bitcast(F32),
                                                ALU.subtract).then_inc(ml_done, 1)
                add_outputs(2 * l, U + MIXER_UNITS)

            def ffn():
                U, F = MIXER_UNITS, DENSE_CHUNKS

                def chunk(f, i=None):
                    split_lo(U + 3 * f + 3 + (f == 0), i)
                    dve.wait_ge(fs_done, at(f + 1, i, FFN_TURN))
                    nc.vector.tensor_tensor(f32_[:, f % 2, :], fs[:, f % 2, :], pa[f % 4][:, T:2 * T],
                                            ALU.mult).then_inc(f32_done, 1)
                    if f:
                        split_lo(U + 3 * f + 4, i)
                    dve.wait_ge(fh_done, at(f + 1, i, FFN_TURN))
                    nc.vector.tensor_tensor(fhl[:, f % 4, :], f32_[:, f % 2, :], fhh[:, f % 4, :].bitcast(F32),
                                            ALU.subtract).then_inc(fl_done, 1)
                    if f < F - 1:
                        split_lo(U + 3 * f + 5, i)
                for f in range(2):
                    chunk(f)
                with dve.Fori(0, FFN_TURNS, 1) as i:
                    for f in range(2, 2 + FFN_TURN):
                        chunk(f, i)
                for f in range(2 + FFN_TURN * FFN_TURNS, F):
                    chunk(f)
                add_outputs(1, U + 3 * F)

            def split_block(i, j):
                dve.wait_ge(hi_done, i * NB + (UNITS + j + 1))
                w = cols(j % NB)
                nc.vector.tensor_tensor(blo[:, j % BSPLIT, 0:w], braw[:, j % BRAW, 0:w],
                                        bhi[:, j % BSPLIT, 0:w].bitcast(F32), ALU.subtract).then_inc(lo_done, 1)

            def tokens():
                for b in range(4):
                    dve.wait_ge(tokh_done, b + 1)
                    at = slice((b // 2) * 512, (b // 2) * 512 + 512)
                    nc.vector.tensor_tensor(htl[:, b % 2, at], TOK[b][:, :], hth[:, b % 2, at].bitcast(F32),
                                            ALU.subtract).then_inc(tokl_done, 1)

            def route():
                lg, mx, ix = small[:, 48:64], small[:, 84:100], small[:, 100:116].bitcast(U32)
                step = [0]

                def then(ins, wait=False):
                    ins.then_inc(top, 1)
                    step[0] += 1
                    if wait:
                        dve.wait_ge(top, step[0])
                dve.wait_ge(logit_done, 1)
                then(nc.vector.tensor_copy(lg, pb[2][:, 48:64]), True)
                for t in range(TT):
                    then(nc.vector.max(mx[:, 8 * t:8 * t + 8], lg[:, 8 * t:8 * t + 8]), t == TT - 1)
                m = mx.rearrange("p (t e) -> p t e", t=TT)
                then(nc.vector.tensor_tensor(small[:, 76:78].rearrange("p (t o) -> p t o", o=1), m[:, :, 1:2],
                                             m[:, :, 0:1], ALU.subtract))
                for t in range(TT):
                    then(nc.vector.max_index(ix[:, 8 * t:8 * t + 8], mx[:, 8 * t:8 * t + 8],
                                             lg[:, 8 * t:8 * t + 8]), t == TT - 1)
                ixf = small[:, 116:120]
                then(nc.vector.tensor_copy(ixf.rearrange("p (k t) -> p t k", k=2),
                                           ix.rearrange("p (t e) -> p t e", t=TT)[:, :, 0:2]), True)
                one, two, chose = small[:, 184:200], small[:, 200:216], small[:, 216:232]
                for t in range(TT):
                    at = slice(8 * t, 8 * t + 8)
                    then(nc.vector.tensor_scalar(one[:, at], expert_no, ixf[:, t:t + 1], None, ALU.is_equal))
                    then(nc.vector.tensor_scalar(two[:, at], expert_no, ixf[:, 2 + t:3 + t], None, ALU.is_equal),
                         t == TT - 1)
                then(nc.vector.tensor_tensor(chose, one, two, ALU.add))
                assert step[0] == CHOSE_AT
                tokens()
                dve.wait_ge(ex_done, 1)
                e = small[:, 80:80 + TT]
                then(nc.vector.tensor_scalar(small[:, 82:84], e, 1.0, None, ALU.add), True)
                wt = small[:, 120:124]
                then(nc.vector.reciprocal(wt[:, 0:2], small[:, 82:84]), True)
                then(nc.vector.tensor_tensor(wt[:, 2:4], wt[:, 0:2], e, ALU.mult), True)
                for t in range(TT):
                    at = slice(8 * t, 8 * t + 8)
                    then(nc.vector.tensor_scalar(one[:, at], one[:, at], wt[:, t:t + 1], None, ALU.mult), t == TT - 1)
                for t in range(TT):
                    at = slice(8 * t, 8 * t + 8)
                    nc_out = gate_of[:, 0:NEXP, t]
                    then(nc.vector.scalar_tensor_tensor(out=nc_out, in0=two[:, at], scalar=wt[:, 2 + t:3 + t],
                                                        in1=one[:, at], op0=ALU.mult, op1=ALU.add))
                dve.wait_ge(pos_done, 1)
                over, rank, junk = small[:, 84:92], small[:, 92:100], small[:, 232:240]
                then(nc.vector.tensor_scalar(over, pb[2][:, 80:88], float(P), None, ALU.is_gt))
                for t in range(TT):
                    at = slice(8 * t, 8 * t + 8)
                    then(nc.vector.scalar_tensor_tensor(out=lg[:, at], in0=pb[2][:, 64 + 8 * t:72 + 8 * t], scalar=1.0,
                                                        in1=chose[:, at], op0=ALU.add, op1=ALU.mult), t == TT - 1)
                for t in range(TT):
                    then(nc.vector.tensor_scalar(slot_of[:, 0:NEXP, t], lg[:, 8 * t:8 * t + 8], -1.0, None, ALU.add),
                         t == TT - 1)
                pick(0)
                then(nc.vector.tensor_tensor_scan(rank, over, over, 0.0, ALU.add, ALU.max), True)
                pf = small[:, 240:244]
                then(nc.vector.tensor_scalar(pf[:, 0:1], rank[:, 7:8], float(NEXP), None, ALU.add))
                for m in range(ITEMS_MOST - NEXP):
                    one8 = small[:, 184 + 8 * m:192 + 8 * m]
                    then(nc.vector.scalar_tensor_tensor(out=one8, in0=rank, scalar=float(m + 1), in1=over,
                                                        op0=ALU.is_equal, op1=ALU.mult), True)
                    then(nc.vector.tensor_tensor_reduce(junk, one8, expert_no, 1.0, 0.0, ALU.mult, ALU.add,
                                                        pf[:, 1 + m:2 + m]), True)
                    for t in range(TT):
                        then(nc.vector.tensor_tensor_reduce(junk, one8, slot_of[:, 0:NEXP, t], 1.0, float(-P), ALU.mult,
                                                            ALU.add, slot_of[:, NEXP + m, t:t + 1]), True)
                        then(nc.vector.tensor_tensor_reduce(junk, one8, gate_of[:, 0:NEXP, t], 1.0, 0.0, ALU.mult,
                                                            ALU.add, gate_of[:, NEXP + m, t:t + 1]), True)
                nc.vector.memset(slot_of[:, ITEMS_MOST, :], -1.0)
                nc.vector.memset(gate_of[:, ITEMS_MOST, :], 0.0)
                nc.vector.tensor_copy(plan, pf).then_inc(plan_done, 1)

            def pick(i):
                for t in range(TT):
                    where = slot_of[:, i, t:t + 1] if isinstance(i, int) else \
                        slot_of[:, bass.ds(i, 1), t:t + 1].rearrange("p i t -> p (i t)")
                    nc.vector.tensor_scalar(sel[:, t, :], slot_no, where, None, ALU.is_equal).then_inc(chosen, 1)

            def rows(i):
                for b in range(2):
                    dve.wait_ge(xgh_done, i * 2 + (b + 1))
                    nc.vector.tensor_tensor(xgl[:, 4 * b:4 * b + 4, :], pb[b][:, :].rearrange("p (c s) -> p c s", c=4),
                                            xgh[:, 4 * b:4 * b + 4, :].bitcast(F32), ALU.subtract).then_inc(xgl_done, 1)

            def outputs(i):
                for b in range(2):
                    dve.wait_ge(yh_done, i * 2 + (b + 1))
                    at = slice(b * 512, (b + 1) * 512)
                    nc.vector.tensor_tensor(ysl[:, at], Y[b][:, :], ysh[:, at].bitcast(F32),
                                            ALU.subtract).then_inc(yl_done, 1)

            def accumulate(i, done):
                for p in range(4):
                    if done is x_done and p >= 2:
                        square_sum(4, p - 2)
                    dve.wait_ge(scat_done, i * 4 + (p + 1))
                    xx = x[:, 2 * p:2 * p + 2, :]
                    nc.vector.tensor_tensor(xx, SCAT[p][:, :].rearrange("p (c t) -> p c t", c=2), xx,
                                            ALU.add).then_inc(done, 1)

            def moe():
                split_block(0, 0)
                route()
                rows(0)
                for j in range(1, BSPLIT - 1):
                    split_block(0, j)
                n = n_items(dve)
                with dve.Fori(0, n, 1) as i:
                    split_block(i, BSPLIT - 1)
                    for j in range(NB):
                        if BLOCKS[j][0] == "w3":
                            gr = BLOCKS[j][1]
                            w = GROUPS[gr] * P
                            dve.wait_ge(unit_done, i * NB + (UNITS + j + 1))
                            dve.wait_ge(fs_done, i * 4 + (FF + gr + 1))
                            nc.vector.scalar_tensor_tensor(out=inner[:, 0:w], in0=act3[:, 0:w], scalar=slot_gate,
                                                           in1=H3[:, 0:w], op0=ALU.mult, op1=ALU.mult).then_inc(f32_done, 1)
                        if j == 1:
                            accumulate(i, x_acc)
                        if j in TURN_AFTER:
                            gr = TURN_AFTER.index(j)
                            w = GROUPS[gr]
                            dve.wait_ge(fh_done, i * 4 + (FF + gr + 1))
                            nc.vector.tensor_tensor(itl[:, gr % 2, 0:w, :],
                                                    pb[3][:, 0:w * P].rearrange("p (c s) -> p c s", c=w),
                                                    ith[:, gr % 2, 0:w, :].bitcast(F32), ALU.subtract).then_inc(fl_done, 1)
                        if j == 9:
                            dve.wait_ge(str_done, i + 1)
                            pick(i + 1)
                        if j == 10:
                            rows(i + 1)
                        if j == NB - 1:
                            outputs(i + 1)
                        else:
                            split_block(i, j + BSPLIT)
                accumulate(n, x_done)

            dve.wait_ge(con_in, 16)
            for c in range(4):
                dve.wait_ge(x_in[c], 16)
            norm(0)
            mixer(0)
            norm(1)
            ffn()
            norm(2)
            mixer(1)
            norm(3)
            moe()
            norm(4)

        @block.tensor
        def _(pe):
            mm = nc.tensor.matmul

            def tiles(u, dst, xh, xl, first, last, turn=None):
                s = u % RING
                pe.wait_ge(hi_done, at(u + 1, turn, FFN_UNITS))
                for i in range(8):
                    w = whi[:, s, i * P:(i + 1) * P]
                    mm(dst(i), w, xh(i), start=first(i), stop=False, skip_group_check=True)
                    mm(dst(i), w, xl(i), start=False, stop=False, skip_group_check=True)
                pe.wait_ge(lo_done, at(u + 1, turn, FFN_UNITS))
                for i in range(8):
                    ins = mm(dst(i), wlo[:, s, i * P:(i + 1) * P], xh(i), start=False, stop=last(i),
                             skip_group_check=True)
                ins.then_inc(unit_done, 1)

            def opening(u, n, dst):
                pe.wait_ge(hi_done, u + 4)

                def part(a, units, made, step, first=False):
                    for i in range(KC):
                        if made is not None and i % step == 0:
                            pe.wait_ge(made, KC // step * n + i // step + 1)
                        for j in units:
                            mm(dst(j), whi[:, (u + j) % RING, i * P:(i + 1) * P], a[:, i, :],
                               start=first and i == 0 and j % 2 == 0, stop=False, skip_group_check=True)
                part(hnh, range(4), nh_done, 1, first=True)
                for pair in ((0, 1), (2, 3)):
                    part(hnl, pair, nl_done if pair[0] == 0 else None, 2)
                    for j in pair:
                        pe.wait_ge(lo_done, u + j + 1)
                        for i in range(KC):
                            ins = mm(dst(j), wlo[:, (u + j) % RING, i * P:(i + 1) * P], hnh[:, i, :], start=False,
                                     stop=i == KC - 1, skip_group_check=True)
                        ins.then_inc(unit_done, 1)

            def into_all(u, ah, al, first, last, turn=None):
                def dst(i):
                    return pb[i // 2][:, (i % 2) * T:(i % 2) * T + T]
                if not last:
                    tiles(u, dst, lambda i: ah, lambda i: al, first=lambda i: first and i % 2 == 0,
                          last=lambda i: False, turn=turn)
                    return
                s = u % RING
                pe.wait_ge(hi_done, u + 1)
                pe.wait_ge(lo_done, u + 1)
                for p in range(4):
                    for i in (2 * p, 2 * p + 1):
                        at = slice(i * P, (i + 1) * P)
                        mm(dst(i), whi[:, s, at], ah, start=False, stop=False, skip_group_check=True)
                        mm(dst(i), whi[:, s, at], al, start=False, stop=False, skip_group_check=True)
                        ins = mm(dst(i), wlo[:, s, at], ah, start=False, stop=True, skip_group_check=True)
                    ins.then_inc(acc_done if p < 3 else unit_done, 1)

            def project(u, dst, ah, al, k0=0, first=True, last=True, turn=None):
                tiles(u, lambda i: dst, lambda i: ah[:, k0 + i, :], lambda i: al[:, k0 + i, :],
                      first=lambda i: first and i == 0, last=lambda i: last and i == 7, turn=turn)

            def keep_warm(n, bank):
                for _ in range(n):
                    mm(bank[:, 0:P], mtmp[:, 0, 0:P], mtmp[:, 0, 0:P], start=True, stop=True)

            def mean(dst, done):
                for c in range(2):
                    ins = mm(dst, mean_of, lsum[:, c, :], start=c == 0, stop=c == 1)
                ins.then_inc(done, 1)

            def spread(dst, per_token, done):
                for t in range(TT):
                    ins = mm(dst[:, t * P:(t + 1) * P], per_token[:, t:t + 1].broadcast_to([P, P]), ident,
                             start=True, stop=True)
                ins.then_inc(done, 1)

            def norm(n):
                if n == 0:
                    pe.wait_ge(warm_zero, 1)
                    keep_warm(WARM_START, pa[1])
                    pe.wait_ge(con_in, 16)
                if n == 4:
                    keep_warm(WARM_END, pa[1])
                for c in range(4):
                    if n == 3:
                        keep_warm(WARM_ROUTER["sum" if c else "first"], pa[1])
                    pe.wait_ge(sum_done, 4 * n + c + 1)
                    for t in range(TT):
                        ins = mm(pa[0][:, t:t + 1], xsum[:, c, t * P:(t + 1) * P], inv_d, start=c == 0 and t == 0,
                                 stop=c == 3, skip_group_check=True)
                ins.then_inc(stat_done, 1)
                if n == 3:
                    keep_warm(WARM_ROUTER["root"], pa[1])
                pe.wait_ge(inv_done, n + 1)
                spread(pa[3][:, 0:T], small[:, 4:4 + TT], bc_done)

            def mixer(l):
                U = LAYER0[l]

                def half(j):
                    return pa[(j // 2) % 4][:, (j % 2) * T:(j % 2) * T + T]

                opening(U + GLU0, 2 * l, half)
                for j in range(4, N_GLU):
                    project(U + GLU0 + j, half(j), hnh, hnl)
                for j in range(N_QK):
                    project(U + QK0 + j, half(j), hnh, hnl)
                for cg in range(4):
                    for j in range(4):
                        u = U + V0 + 4 * cg + j
                        s = u % RING
                        pe.wait_ge(hi_done, u + 1)
                        for part in range(2):
                            if part:
                                pe.wait_ge(lo_done, u + 1)
                            for kk in range(2):
                                w = (wlo if part else whi)[:, s, kk * 512:(kk + 1) * 512]
                                for t in range(TT):
                                    dst = pa[(2 * cg + t) % 4][:, :]
                                    for a in ((hnh,) if part else (hnh, hnl)):
                                        ins = mm(dst, a[:, 2 * j + kk, t * P:(t + 1) * P], w,
                                                 start=j == 0 and kk == 0 and part == 0 and a is hnh,
                                                 stop=j == 3 and part == 1 and kk == 1, skip_group_check=True)
                        ins.then_inc(unit_done, 1)
                pe.wait_ge(qk_done, 16 * l + 16)
                for h in range(HEADS):
                    for t in range(TT):
                        n0, dst = t * P, pb[h][:, 0:T] if t == 0 else pb[h][:, T:SCW]
                        for c in range(2):
                            ins = mm(dst, k[:, h, c * T + t * P:c * T + (t + 1) * P], q[:, h, c * T + n0:(c + 1) * T],
                                     start=c == 0, stop=c == 1)
                    ins.then_inc(score_done, 1)

                def pv(h):
                    pe.wait_ge(prob_done, 4 * l + 4)
                    pe.wait_ge(v_done, 2 * (4 * l + h + 1))
                    if h:
                        pe.wait_ge(rg_done, 8 * l + 2 * h)
                        pe.wait_ge(rsq_done, 8 * l + 2 * h)
                    for e in range(4):
                        dst = pb[e // 2]
                        o = (e % 2) * T
                        mm(dst[:, o:o + T], v[:, h, 0, e * P:(e + 1) * P], prob[:, h, 0:T], start=True, stop=True)
                        ins = mm(dst[:, o + P:o + T], v[:, h, 1, e * P:(e + 1) * P], prob[:, h, T:SCW], start=False,
                                 stop=True, skip_group_check=True)
                    ins.then_inc(pv_done, 1)

                def rstat(h):
                    pe.wait_ge(rsum_done, 4 * l + h + 1)
                    for t in range(TT):
                        for c in range(2):
                            ins = mm(pb[2][:, 8 + 2 * h + t:9 + 2 * h + t], rsq[:, h % 2, c, t * P:(t + 1) * P], inv_v,
                                     start=c == 0, stop=c == 1)
                    ins.then_inc(rstat_done, 1)
                for p in range(8):
                    project(U + G0 + 2 * p, half(2 * p), hnh, hnl)
                    project(U + G0 + 2 * p + 1, half(2 * p + 1), hnh, hnl)
                    if p % 2:
                        pv(p // 2)
                    if p in (4, 6):
                        rstat((p - 4) // 2)
                for p in range(8):
                    project(U + MG0 + 2 * p, half(2 * p), hnh, hnl)
                    if p == 4:
                        pe.wait_ge(rg_done, 8 * l + 8)
                        pe.wait_ge(rsq_done, 8 * l + 8)
                        pe.wait_ge(rinv_done, l + 1)
                        for h in range(HEADS):
                            spread(pb[h // 2][:, (h % 2) * T:(h % 2) * T + T], small[:, 16 + 2 * h:18 + 2 * h], rbc_done)
                    project(U + MG0 + 2 * p + 1, half(2 * p + 1), hnh, hnl)
                    if p < 2:
                        rstat(2 + p)
                for j in range(N_RO):
                    c, part = 2 * (j // 4) + j % 2, (j % 4) // 2
                    if j in (0, 2):
                        pe.wait_ge(rh_done, 4 * l + 2 + j)
                        pe.wait_ge(rl_done, 4 * l + 2 + j)
                    project(U + RO0 + j, pa[c % 4][:, 0:T], rh, rl, k0=8 * part, first=part == 0, last=part == 1)
                    if j == LN_MEAN + 1:
                        pe.wait_ge(lsum1, 2 * l + 2)
                        mean(pb[2][:, 0:T], lmean)
                    if j == LN_VAR:
                        pe.wait_ge(lsum2, 2 * l + 2)
                        mean(pb[3][:, 0:T], lstat)
                pe.wait_ge(uh_done, 4 * l + 4)
                pe.wait_ge(ul_done, 4 * l + 4)
                for n, (what, c) in enumerate(TAIL):
                    u = U + TAIL0 + n
                    if what == "co":
                        if c >= 4:
                            pe.wait_ge(mstep, 3 * (8 * l + c - 4) + 1)
                        else:
                            pe.wait_ge(gated_done, 8 * l + c + 5)
                        project(u, pa[c % 4][:, 0:T], uh, ul)
                    else:
                        pe.wait_ge(mh_done, 8 * l + c + 1)
                        pe.wait_ge(ml_done, 8 * l + c + 1)
                        into_all(u, mh[:, c, :], ml[:, c, :], first=c == 0, last=c == N_WO - 1)

            def ffn():
                U, F = MIXER_UNITS, DENSE_CHUNKS

                def up(f, i=None):
                    u = U + 3 * f - 1
                    project(u, pa[f % 4][:, 0:T], hnh, hnl, turn=i)
                    project(u + 1, pa[f % 4][:, T:2 * T], hnh, hnl, turn=i)

                def down(f, i=None):
                    u = U + 3 * f + 4 - 2 * (f == F - 1)
                    pe.wait_ge(fh_done, at(f + 1, i, FFN_TURN))
                    pe.wait_ge(fl_done, at(f + 1, i, FFN_TURN))
                    into_all(u, fhh[:, f % 4, :], fhl[:, f % 4, :], first=f == 0, last=f == F - 1, turn=i)
                opening(U, 1, lambda j: pa[j // 2][:, (j % 2) * T:(j % 2) * T + T])
                down(0)
                with pe.Fori(0, FFN_TURNS, 1) as i:
                    for f in range(2, 2 + FFN_TURN):
                        up(f, i)
                        down(f - 1, i)
                for f in range(2 + FFN_TURN * FFN_TURNS, F):
                    up(f)
                    down(f - 1)
                down(F - 1)

            def route():
                keep_warm(WARM_ROUTER["rows"], pa[1])
                pe.wait_ge(x_done, 12)
                for c in range(KC):
                    pe.wait_ge(n32_done, 8 * 3 + c + 1)
                    for t in range(TT):
                        ins = mm(pb[2][:, 48 + 8 * t:56 + 8 * t], hn32[:, c, t * P:(t + 1) * P],
                                 con[:, C_ROUT + c * NEXP:C_ROUT + (c + 1) * NEXP], start=c == 0 and t == 0,
                                 stop=c == KC - 1, skip_group_check=True)
                    if c == KC - 1:
                        ins.then_inc(logit_done, 1)
                    for t in range(TT):
                        ins = nc.tensor.transpose(TOK[c // 4 * 2 + t][:, (c % 4) * P:(c % 4 + 1) * P],
                                                  hn32[:, c, t * P:(t + 1) * P], ident)
                    if c % 4 == 3:
                        ins.then_inc(tok_tr, 1)
                pe.wait_ge(top, CHOSE_AT)
                chose = small[:, 216:232]
                at = [pb[2][:, 64 + 8 * i:72 + 8 * i] for i in range(3)]
                mm(at[0], before, chose[:, 0:8], start=True, stop=True)
                mm(at[1], ones, chose[:, 0:8], start=True, stop=False)
                mm(at[1], before, chose[:, 8:16], start=False, stop=True)
                mm(at[2], ones, chose[:, 0:8], start=True, stop=False)
                mm(at[2], ones, chose[:, 8:16], start=False, stop=True).then_inc(pos_done, 1)
                keep_warm(WARM_SLOTS, pa[0])

            def gather(i):
                for c in range(KC):
                    dst = pb[c // 4][:, (c % 4) * P:(c % 4 + 1) * P]
                    for t in range(TT):
                        mm(dst, hth[:, t, c * P:(c + 1) * P], sel[:, t, :], start=t == 0, stop=False)
                        mm(dst, htl[:, t, c * P:(c + 1) * P], sel[:, t, :], start=False, stop=t == TT - 1)
                for t in range(TT):
                    gate = gate_of[:, i, t:t + 1] if isinstance(i, int) else \
                        gate_of[:, bass.ds(i, 1), t:t + 1].rearrange("p i t -> p (i t)")
                    ins = mm(pb[2][:, 0:1], sel[:, t, :].bitcast(F32), gate, start=t == 0, stop=t == TT - 1)
                ins.then_inc(gath_done, 1)

            def scatter(i):
                pe.wait_ge(yh_done, i * 2 + 2)
                pe.wait_ge(yl_done, i * 2 + 2)
                pe.wait_ge(st_done, i + 1)
                for p in range(4):
                    for c in (2 * p, 2 * p + 1):
                        dst = SCAT[p][:, (c % 2) * T:(c % 2) * T + T]
                        mm(dst, ysh[:, c * P:(c + 1) * P], selt[:, :], start=True, stop=False)
                        ins = mm(dst, ysl[:, c * P:(c + 1) * P], selt[:, :], start=False, stop=True)
                    ins.then_inc(scat_done, 1)

            def block_up(i, j):
                s, w = j % BSPLIT, GROUPS[BLOCKS[j][1]] * P
                dst = (H1 if BLOCKS[j][0] == "w1" else H3)[:, 0:w]
                pe.wait_ge(hi_done, i * NB + (UNITS + j + 1))
                for c in range(KC):
                    mm(dst, xgh[:, c, :], bhi[:, s, c * w:(c + 1) * w], start=c == 0, stop=False)
                    mm(dst, xgl[:, c, :], bhi[:, s, c * w:(c + 1) * w], start=False, stop=False)
                pe.wait_ge(lo_done, i * NB + (UNITS + j + 1))
                for c in range(KC):
                    ins = mm(dst, xgh[:, c, :], blo[:, s, c * w:(c + 1) * w], start=False, stop=c == KC - 1)
                ins.then_inc(unit_done, 1)

            def block_down(i, j):
                s, gr = j % BSPLIT, BLOCKS[j][1]
                pe.wait_ge(fh_done, i * 4 + (FF + gr + 1))
                pe.wait_ge(fl_done, i * 4 + (FF + gr + 1))
                if gr == 0:
                    pe.wait_ge(x_acc, i * 4 + 4)
                pe.wait_ge(hi_done, i * NB + (UNITS + j + 1))
                for part in range(2):
                    if part:
                        pe.wait_ge(lo_done, i * NB + (UNITS + j + 1))
                    for c in range(GROUPS[gr]):
                        for b in range(2):
                            w = (blo if part else bhi)[:, s, c * D + b * 512:c * D + (b + 1) * 512]
                            for a in ((ith,) if part else (ith, itl)):
                                ins = mm(Y[b][:, :], a[:, gr % 2, c, :], w, start=gr == 0 and c == 0 and a is ith and not part,
                                         stop=gr == 3 and part == 1 and c == GROUPS[gr] - 1, skip_group_check=True)
                ins.then_inc(unit_done, 1)

            def turn(i, gr):
                pe.wait_ge(f32_done, i * 4 + (FF + gr + 1))
                pe.wait_ge(fl_done, i * 4 + (FF + gr))
                if gr == 0:
                    pe.wait_ge(st_done, i + 2)
                for c in range(GROUPS[gr]):
                    ins = nc.tensor.transpose(pb[3][:, c * P:(c + 1) * P], inner[:, c * P:(c + 1) * P], ident)
                ins.then_inc(trh_done, 1)

            def moe():
                route()
                pe.wait_ge(tokl_done, 4)
                pe.wait_ge(chosen, 2)
                gather(0)
                n = n_items(pe)
                with pe.Fori(0, n, 1) as i:
                    for j in range(NB):
                        if j == 0:
                            pe.wait_ge(xgh_done, i * 2 + 2)
                            pe.wait_ge(xgl_done, i * 2 + 2)
                        if j == 11:
                            turn(i, 3)
                            pe.wait_ge(chosen, i * 2 + 4)
                            pe.wait_ge(x_acc, i * 4 + 4)
                            gather(i + 1)
                        if BLOCKS[j][0] == "w1":
                            if j:
                                pe.wait_ge(fs_done, i * 4 + (FF + BLOCKS[j][1]))
                        if BLOCKS[j][0] == "w3":
                            if j > 1:
                                pe.wait_ge(f32_done, i * 4 + (FF + BLOCKS[j][1]))
                        (block_down if BLOCKS[j][0] == "w2" else block_up)(i, j)
                        if j == 1:
                            scatter(i)
                            for t in range(TT):
                                ins = nc.tensor.transpose(pb[3][:, t * P:(t + 1) * P], sel[:, t, :].bitcast(F32), ident)
                            ins.then_inc(str_done, 1)
                        if j in TURN_AFTER[0:3]:
                            turn(i, TURN_AFTER.index(j))
                scatter(n)

            norm(0)
            mixer(0)
            norm(1)
            ffn()
            norm(2)
            mixer(1)
            norm(3)
            moe()
            norm(4)


def columns(w):
    kk, n = w.shape
    w = w.reshape(kk // D, KC, P, n // P, P)
    return w.transpose(3, 0, 2, 1, 4).reshape(-1, P, UNIT)


def wide(w):
    w = w.reshape(4, 2, P, w.shape[1] // 512, 512)
    return w.transpose(3, 0, 2, 1, 4).reshape(-1, P, UNIT)


def kernel(**inputs):
    import concourse.bacc as bacc
    from concourse.bass_utils import run_bass_kernel_spmd as run

    a = {n: np.asarray(v) for n, v in inputs.items()}

    def pairs(u, w):
        return np.stack([u, w], 1).reshape(-1, P, UNIT)

    wts = np.empty((UNITS, P, UNIT), np.float32)
    for l in range(DEPTH):
        U = LAYER0[l]
        w_in = a["w_in"][l]
        cut = np.cumsum([0, D, D, VW, VW, D, D, D, D])
        wq, wk, wv, wg, wval, wgate, wga, wgb = (w_in[:, cut[i]:cut[i + 1]] for i in range(8))
        wts[U + GLU0:U + QK0] = pairs(columns(wval), columns(wgate))
        wts[U + QK0:U + V0] = np.concatenate([columns(wq), columns(wk)])
        wts[U + V0:U + G0] = wide(wv)
        wts[U + G0:U + MG0] = columns(wg)
        wts[U + MG0:U + RO0] = pairs(columns(wga), columns(wgb))
        ro = columns(a["w_ret_o"][l]).reshape(KC // 2, 2, 2, P, UNIT)
        wts[U + RO0:U + TAIL0] = ro.transpose(0, 2, 1, 3, 4).reshape(-1, P, UNIT)
        wts[[U + TAIL0 + TAIL.index(("co", c)) for c in range(N_CO)]] = columns(a["w_conv_o"][l])
        wts[[U + TAIL0 + TAIL.index(("wo", c)) for c in range(N_WO)]] = a["w_out"][l].reshape(-1, P, UNIT)
        if l == 0:
            f = np.arange(DENSE_CHUNKS)
            at = U + MIXER_UNITS
            wts[at + 3 * f - (f > 0)] = columns(a["dense_w1"][0])
            wts[at + 3 * f + 1 - (f > 0)] = columns(a["dense_w3"][0])
            wts[at + 3 * (f + 1) + 1 - 2 * (f == DENSE_CHUNKS - 1)] = a["dense_w2"][0].reshape(-1, P, UNIT)
    big = np.empty((NEXP, len(BIG_OF), P, BIG), np.float32)
    last_group = np.empty((NEXP, len(LAST_OF), P, LAST), np.float32)
    for b in BLOCKS:
        n0, w = sum(GROUPS[:b[1]]) * P, GROUPS[b[1]] * P
        m = a["moe_" + b[0]][0]
        if b[0] == "w2":
            m = m[:, n0:n0 + w].reshape(NEXP, w // P, P, D)
        else:
            m = m[:, :, n0:n0 + w].reshape(NEXP, KC, P, w)
        m = m.transpose(0, 2, 1, 3).reshape(NEXP, P, -1)
        if b[1] < 3:
            big[:, BIG_OF[b]] = m
        else:
            last_group[:, LAST_OF[b]] = m

    con = np.zeros((P, C_END), np.float32)
    half = QKD // 2
    inv_freq = np.float32(10000.0) ** (-np.arange(half, dtype=np.float32) / np.float32(half))
    ang = (np.arange(T, dtype=np.float32)[None, :] * inv_freq[:, None]).astype(np.float32)
    con[:, C_COS:C_COS + 2 * T] = np.tile(np.cos(ang), 2)
    con[:, C_SIN:C_SIN + 2 * T] = np.tile(np.sin(ang), 2)
    log_g = np.log1p(-np.exp2(-5.0 - np.arange(HEADS)))
    n, m = np.arange(T)[None, :], np.arange(T)[:, None]
    seen = n // CHUNK >= m // CHUNK
    for h in range(HEADS):
        dec = np.where(seen, np.exp(log_g[h] * np.abs(n - m)), 0.0) * QKD ** -0.5
        at = C_DEC + h * SCW
        con[:, at:at + T] = dec[0:P]
        con[:, at + T:at + SCW] = dec[P:, P:]
    con[:, C_IDENT:C_IDENT + P] = np.eye(P)
    con[:, C_ONES:C_ONES + P] = 1.0
    con[:, C_CW:C_ROUT] = a["conv_w"].reshape(DEPTH, TAPS, KC, P).transpose(3, 0, 2, 1).reshape(P, -1)
    bg = a["b_gate"]
    vecs = [a["mix_norm"], a["conv_b"], a["conv_ln_g"], a["conv_ln_b"], bg[:, :D], bg[:, D:], a["b_conv_o"], a["ffn_norm"]]
    for i, w in enumerate(vecs):
        for l in range(DEPTH):
            at = C_VEC + (l * len(VECS) + i) * KC
            con[:, at:at + KC] = w[l].reshape(KC, P).T
    con[:, C_FIN:C_FIN + KC] = a["final_norm"].reshape(KC, P).T
    con[:, C_ROUT:C_TRI] = a["moe_router"][0].reshape(KC, P, NEXP).transpose(1, 0, 2).reshape(P, -1)
    con[:, C_SM] = 1.0 / D
    con[:, C_SM + 1] = 1.0 / VD
    con[:, C_SM + 2] = EPS
    con[:, C_SM + 3:C_LATER] = np.arange(NEXP)
    con[:, C_TRI:C_IOTA] = np.triu(np.ones((P, P)), 1)
    con[:, C_IOTA:C_COS] = np.arange(P)
    xt = np.ascontiguousarray(a["x"].reshape(T, KC, P).transpose(2, 1, 0))

    nc = bacc.Bacc("TRN2", target_bir_lowering=False, num_devices=1)
    feeds = {"xt": xt, "wts": wts, "big": big, "last_group": last_group, "consts": con}
    args = [nc.dram_tensor(n, v.shape, F32, kind="ExternalInput").ap() for n, v in feeds.items()]
    args.append(nc.dram_tensor("out", (P, KC, T), F32, kind="ExternalOutput").ap())
    build(nc, *args)
    r = run(nc, [feeds], core_ids=[0])
    return np.asarray(r.results[0]["out"]).transpose(2, 1, 0).reshape(1, T, D)
```
